# Optimizing a Trainium2 kernel written in Bass

```python
import math
import jax, jax.numpy as jnp
from jax import lax
import numpy as np

D_MODEL = 1024
BATCH = 1
SEQ = 512
DEPTH = 1

GDN_HEADS = 8
GDN_DK = 128
GDN_DV = 128
SSD_HEADS = 16
SSD_HEADDIM = 64
SSD_GROUPS = 2
SSD_STATE = 128
CONV_K = 4
CHUNK = 64
D_FF = 2816
FFN_CONV_K = 3
EPS = 1e-6

GDN_QK = GDN_HEADS * GDN_DK
GDN_V = GDN_HEADS * GDN_DV
SSD_D = SSD_HEADS * SSD_HEADDIM
SSD_BC = SSD_GROUPS * SSD_STATE
SSD_HPG = SSD_HEADS // SSD_GROUPS
MIX_WIDTH = GDN_V + SSD_D
GDN_CONV_CH = 2 * GDN_QK + GDN_V
SSD_CONV_CH = SSD_D + 2 * SSD_BC
IN_SPLITS = (GDN_QK, GDN_QK, GDN_V, GDN_V, GDN_HEADS, GDN_HEADS,
             SSD_D, SSD_D, SSD_BC, SSD_BC, SSD_HEADS)
D_IN_PROJ = sum(IN_SPLITS)


def rms_norm(x, w):
    xf = x.astype(jnp.float32)
    y = xf * lax.rsqrt(jnp.mean(xf * xf, axis=-1, keepdims=True) + EPS)
    return (y * w.astype(jnp.float32)).astype(x.dtype)

def l2_normalize(x):
    xf = x.astype(jnp.float32)
    return xf * lax.rsqrt(jnp.sum(xf * xf, axis=-1, keepdims=True) + EPS)

def causal_dwconv(x, w, b=None):
    k_w, ch = w.shape
    y = lax.conv_general_dilated(
        x, w[:, None, :].astype(x.dtype), window_strides=(1,), padding=[(k_w - 1, 0)],
        dimension_numbers=("NWC", "WIO", "NWC"), feature_group_count=ch)
    if b is not None:
        y = y + b.astype(x.dtype)
    return y

def gdn_chunked(q, k, v, g, beta):
    bsz, s, h, dk = q.shape
    dv = v.shape[-1]
    n = s // CHUNK

    def chunk(t):
        return jnp.moveaxis(t.reshape(bsz, n, CHUNK, h, *t.shape[3:]), 3, 1)

    q, k, v, g, beta = (chunk(t) for t in (q, k, v, g, beta))
    gc = jnp.cumsum(g, axis=-1)
    causal = jnp.tril(jnp.ones((CHUNK, CHUNK), dtype=bool))
    strict = jnp.tril(jnp.ones((CHUNK, CHUNK), dtype=bool), -1)
    decay = jnp.exp(jnp.where(causal, gc[..., :, None] - gc[..., None, :], -jnp.inf))
    kb = k * beta[..., None]
    a_in = jnp.einsum("bhnid,bhnjd->bhnij", kb, k) * decay
    lmat = jnp.where(strict, a_in, 0.0) + jnp.eye(CHUNK, dtype=a_in.dtype)
    rhs = jnp.concatenate([v * beta[..., None], kb * jnp.exp(gc)[..., None]], axis=-1)
    sol = lax.linalg.triangular_solve(lmat, rhs, left_side=True, lower=True, unit_diagonal=True)
    u, w = sol[..., :dv], sol[..., dv:]
    qk = jnp.einsum("bhnid,bhnjd->bhnij", q, k) * decay
    q_dec = q * jnp.exp(gc)[..., None]
    k_dec = k * jnp.exp(gc[..., -1:] - gc)[..., None]
    g_last = jnp.exp(gc[..., -1])

    def step(state, xs):
        u_i, w_i, qk_i, q_i, k_i, gl = xs
        v_new = u_i - jnp.einsum("bhcd,bhde->bhce", w_i, state)
        o = jnp.einsum("bhcd,bhde->bhce", q_i, state) + jnp.einsum("bhij,bhje->bhie", qk_i, v_new)
        state = state * gl[..., None, None] + jnp.einsum("bhcd,bhce->bhde", k_i, v_new)
        return state, o

    xs = tuple(jnp.moveaxis(t, 2, 0) for t in (u, w, qk, q_dec, k_dec, g_last))
    s0 = jnp.zeros((bsz, h, dk, dv), dtype=q.dtype)
    _, o = lax.scan(step, s0, xs)
    return jnp.transpose(o, (1, 0, 3, 2, 4)).reshape(bsz, s, h, dv)

def ssd_chunked(x, dt, a_neg, bmat, cmat):
    bsz, s, grp, hg, p = x.shape
    nst = bmat.shape[-1]
    n = s // CHUNK
    xdt = x * dt[..., None]
    adt = dt * a_neg

    def chunk(t):
        return jnp.moveaxis(t.reshape(bsz, n, CHUNK, *t.shape[2:]), 1, 0)

    xs = tuple(chunk(t) for t in (xdt, adt, bmat, cmat))
    causal = jnp.tril(jnp.ones((CHUNK, CHUNK), dtype=bool))

    def step(state, xs):
        xdt_i, adt_i, b_i, c_i = xs
        acs = jnp.cumsum(jnp.moveaxis(adt_i, 1, -1), axis=-1)
        lmat = jnp.exp(jnp.where(causal, acs[..., :, None] - acs[..., None, :], -jnp.inf))
        cb = jnp.einsum("blgn,bsgn->bgls", c_i, b_i)
        y_diag = jnp.einsum("bgls,bghls,bsghp->blghp", cb, lmat, xdt_i)
        y_off = jnp.einsum("blgn,bghpn,bghl->blghp", c_i, state, jnp.exp(acs))
        decay_s = jnp.exp(acs[..., -1:] - acs)
        state = state * jnp.exp(acs[..., -1])[..., None, None] + jnp.einsum(
            "bsgn,bghs,bsghp->bghpn", b_i, decay_s, xdt_i)
        return state, y_diag + y_off

    s0 = jnp.zeros((bsz, grp, hg, p, nst), dtype=x.dtype)
    _, y = lax.scan(step, s0, xs)
    return jnp.moveaxis(y, 0, 1).reshape(bsz, s, grp, hg, p)

def hybrid_layer(x, pre_mix_norm, w_in, gdn_conv_w, gdn_a_log, gdn_dt_bias, gdn_norm_w,
                 ssd_conv_w, ssd_conv_b, ssd_a_log, ssd_dt_bias, ssd_d, ssd_norm_w,
                 w_out, post_mix_norm, pre_ffn_norm, w_up, ffn_conv_w, ffn_conv_b,
                 w_down, post_ffn_norm):
    f32 = jnp.float32
    bsz, s, _ = x.shape
    h = rms_norm(x, pre_mix_norm)
    proj = h @ w_in
    offsets = np.cumsum(IN_SPLITS)[:-1].tolist()
    q, k, v, z_a, b_a, a_a, z_s, x_s, b_s, c_s, dt_s = jnp.split(proj, offsets, axis=-1)

    qkv = jax.nn.silu(causal_dwconv(jnp.concatenate([q, k, v], axis=-1), gdn_conv_w))
    q, k, v = jnp.split(qkv, [GDN_QK, 2 * GDN_QK], axis=-1)
    q = l2_normalize(q.reshape(bsz, s, GDN_HEADS, GDN_DK)) * (GDN_DK ** -0.5)
    k = l2_normalize(k.reshape(bsz, s, GDN_HEADS, GDN_DK))
    v = v.reshape(bsz, s, GDN_HEADS, GDN_DV).astype(f32)
    beta = jax.nn.sigmoid(b_a.astype(f32))
    g = -jnp.exp(gdn_a_log.astype(f32)) * jax.nn.softplus(a_a.astype(f32) + gdn_dt_bias.astype(f32))
    o_a = gdn_chunked(q, k, v, g, beta)
    o_a = rms_norm(o_a, gdn_norm_w) * jax.nn.silu(z_a.reshape(bsz, s, GDN_HEADS, GDN_DV).astype(f32))
    o_a = o_a.reshape(bsz, s, GDN_V).astype(x.dtype)

    xbc = jax.nn.silu(causal_dwconv(jnp.concatenate([x_s, b_s, c_s], axis=-1), ssd_conv_w, ssd_conv_b))
    xs_, bm, cm = jnp.split(xbc, [SSD_D, SSD_D + SSD_BC], axis=-1)
    xs_ = xs_.reshape(bsz, s, SSD_GROUPS, SSD_HPG, SSD_HEADDIM).astype(f32)
    bm = bm.reshape(bsz, s, SSD_GROUPS, SSD_STATE).astype(f32)
    cm = cm.reshape(bsz, s, SSD_GROUPS, SSD_STATE).astype(f32)
    dt = jax.nn.softplus(dt_s.astype(f32) + ssd_dt_bias.astype(f32)).reshape(bsz, s, SSD_GROUPS, SSD_HPG)
    a_neg = -jnp.exp(ssd_a_log.astype(f32)).reshape(SSD_GROUPS, SSD_HPG)
    y = ssd_chunked(xs_, dt, a_neg, bm, cm)
    y = y + ssd_d.astype(f32).reshape(SSD_GROUPS, SSD_HPG)[..., None] * xs_
    y = y.reshape(bsz, s, SSD_D) * jax.nn.silu(z_s.astype(f32))
    y = rms_norm(y.reshape(bsz, s, SSD_GROUPS, SSD_D // SSD_GROUPS),
                 ssd_norm_w.reshape(SSD_GROUPS, SSD_D // SSD_GROUPS))
    o_s = y.reshape(bsz, s, SSD_D).astype(x.dtype)

    mix = jnp.concatenate([o_a, o_s], axis=-1) @ w_out
    x = x + rms_norm(mix, post_mix_norm)

    h = rms_norm(x, pre_ffn_norm)
    u = causal_dwconv(h @ w_up, ffn_conv_w, ffn_conv_b)
    gate, up = jnp.split(u, 2, axis=-1)
    f = (jax.nn.silu(gate) * up) @ w_down
    return x + rms_norm(f, post_ffn_norm)

def first_inputs(seed: int = 0) -> dict:
    key = jax.random.key(seed)
    ks = jax.random.split(key, 24)
    f32 = jnp.float32
    L = DEPTH

    def nrm(k, shape, scale):
        return jax.random.normal(k, shape, f32) * scale

    def gain(k, shape):
        return 1.0 + 0.05 * jax.random.normal(k, shape, f32)

    def dt_bias(k, shape):
        dt = jnp.exp(jax.random.uniform(k, shape, f32, math.log(1e-3), math.log(1e-1)))
        return dt + jnp.log(-jnp.expm1(-dt))

    def a_log(k, shape):
        return jnp.log(jax.random.uniform(k, shape, f32, 1.0, 16.0))

    return {
        "x": nrm(ks[0], (BATCH, SEQ, D_MODEL), 1.0),
        "pre_mix_norm": gain(ks[1], (L, D_MODEL)),
        "w_in": nrm(ks[2], (L, D_MODEL, D_IN_PROJ), D_MODEL ** -0.5),
        "gdn_conv_w": nrm(ks[3], (L, CONV_K, GDN_CONV_CH), CONV_K ** -0.5),
        "gdn_a_log": a_log(ks[4], (L, GDN_HEADS)),
        "gdn_dt_bias": dt_bias(ks[5], (L, GDN_HEADS)),
        "gdn_norm_w": gain(ks[6], (L, GDN_DV)),
        "ssd_conv_w": nrm(ks[7], (L, CONV_K, SSD_CONV_CH), CONV_K ** -0.5),
        "ssd_conv_b": nrm(ks[8], (L, SSD_CONV_CH), 0.02),
        "ssd_a_log": a_log(ks[9], (L, SSD_HEADS)),
        "ssd_dt_bias": dt_bias(ks[10], (L, SSD_HEADS)),
        "ssd_d": gain(ks[11], (L, SSD_HEADS)),
        "ssd_norm_w": gain(ks[12], (L, SSD_D)),
        "w_out": nrm(ks[13], (L, MIX_WIDTH, D_MODEL), MIX_WIDTH ** -0.5),
        "post_mix_norm": gain(ks[14], (L, D_MODEL)),
        "pre_ffn_norm": gain(ks[15], (L, D_MODEL)),
        "w_up": nrm(ks[16], (L, D_MODEL, 2 * D_FF), D_MODEL ** -0.5),
        "ffn_conv_w": nrm(ks[17], (L, FFN_CONV_K, 2 * D_FF), FFN_CONV_K ** -0.5),
        "ffn_conv_b": nrm(ks[18], (L, 2 * D_FF), 0.02),
        "w_down": nrm(ks[19], (L, D_FF, D_MODEL), D_FF ** -0.5),
        "post_ffn_norm": gain(ks[20], (L, D_MODEL)),
    }

def first_block(x, pre_mix_norm, w_in, gdn_conv_w, gdn_a_log, gdn_dt_bias, gdn_norm_w,
              ssd_conv_w, ssd_conv_b, ssd_a_log, ssd_dt_bias, ssd_d, ssd_norm_w,
              w_out, post_mix_norm, pre_ffn_norm, w_up, ffn_conv_w, ffn_conv_b,
              w_down, post_ffn_norm):
    for l in range(DEPTH):
        x = hybrid_layer(x, pre_mix_norm[l], w_in[l], gdn_conv_w[l], gdn_a_log[l], gdn_dt_bias[l],
                         gdn_norm_w[l], ssd_conv_w[l], ssd_conv_b[l], ssd_a_log[l], ssd_dt_bias[l],
                         ssd_d[l], ssd_norm_w[l], w_out[l], post_mix_norm[l], pre_ffn_norm[l],
                         w_up[l], ffn_conv_w[l], ffn_conv_b[l], w_down[l], post_ffn_norm[l])
    return x


GRID_W = 64
CTX_LEN = 256
N_FOURIER_GROUPS = 4
FOURIER_GROUP_DIM = 128
FOURIER_WIDTH = N_FOURIER_GROUPS * FOURIER_GROUP_DIM
NA_HEADS = 8
HEAD_DIM = 64
NA_WIDTH = NA_HEADS * HEAD_DIM
IN_WIDTH = FOURIER_WIDTH + 3 * NA_WIDTH
WIN_ROWS = 8
WIN_COLS = 16
N_BRANCHES = 2
D_FF_2 = 4 * D_MODEL
ROPE_THETA = 10000.0
NORM_EPS = 1e-6
N_MOD = 6


def rms_norm_2(x, g):
    xf = x.astype(jnp.float32)
    y = xf * lax.rsqrt(jnp.mean(xf * xf, axis=-1, keepdims=True) + NORM_EPS)
    return (y * g.astype(jnp.float32)).astype(x.dtype)

def modulate(h, shift, scale):
    return h * (1 + scale) + shift

def ada_mod(cond, w, b):
    m = jax.nn.silu(cond) @ w + b
    return jnp.split(m, N_MOD, axis=-1)

def split_heads(a):
    return a.reshape(a.shape[0], a.shape[1], NA_HEADS, HEAD_DIM)

def split_projection(p):
    f = p[..., :FOURIER_WIDTH]
    q = p[..., FOURIER_WIDTH:FOURIER_WIDTH + NA_WIDTH]
    k = p[..., FOURIER_WIDTH + NA_WIDTH:FOURIER_WIDTH + 2 * NA_WIDTH]
    v = p[..., FOURIER_WIDTH + 2 * NA_WIDTH:]
    return f, split_heads(q), split_heads(k), split_heads(v)

def rope_1d(x, cos, sin):
    m = x.shape[-1] // 2
    x1, x2 = x[..., :m], x[..., m:]
    cos = cos[None, :, None, :]
    sin = sin[None, :, None, :]
    return jnp.concatenate([x1 * cos - x2 * sin, x1 * sin + x2 * cos], axis=-1)

def axial_rope(x):
    n_tok = x.shape[1]
    t = jnp.arange(n_tok)
    row = (t // GRID_W).astype(jnp.float32)
    col = (t % GRID_W).astype(jnp.float32)
    axis_dim = HEAD_DIM // 2
    inv_freq = ROPE_THETA ** (-jnp.arange(0, axis_dim, 2, dtype=jnp.float32) / axis_dim)
    ang_r = row[:, None] * inv_freq
    ang_c = col[:, None] * inv_freq
    xf = x.astype(jnp.float32)
    xr = rope_1d(xf[..., :axis_dim], jnp.cos(ang_r), jnp.sin(ang_r))
    xc = rope_1d(xf[..., axis_dim:], jnp.cos(ang_c), jnp.sin(ang_c))
    return jnp.concatenate([xr, xc], axis=-1).astype(x.dtype)

def fourier_mix(u):
    b, n, _ = u.shape
    ug = u.astype(jnp.float32).reshape(b, n, N_FOURIER_GROUPS, FOURIER_GROUP_DIM)
    y = jnp.fft.fft2(ug, axes=(1, 3), norm="ortho").real
    return y.reshape(b, n, FOURIER_WIDTH).astype(u.dtype)

def neighbourhood_attention(q, k, v, k_ctx, v_ctx, rpb):
    b, s, h, dh = q.shape
    rows = s // GRID_W
    kr = min(WIN_ROWS, rows)
    kc = WIN_COLS
    n_loc = kr * kc
    scale = dh ** -0.5
    qg = q.reshape(b, rows, GRID_W, h, dh)
    kg = k.reshape(b, rows, GRID_W, h, dh)
    vg = v.reshape(b, rows, GRID_W, h, dh)
    r = jnp.arange(rows)
    cc = jnp.arange(GRID_W)
    row_start = jnp.clip(r - kr // 2, 0, rows - kr)
    col_start = jnp.clip(cc - kc // 2, 0, GRID_W - kc)
    col_idx = col_start[:, None] + jnp.arange(kc)
    dc_idx = col_idx - cc[:, None] + (WIN_COLS - 1)
    dr_idx = row_start[:, None] + jnp.arange(kr) - r[:, None] + (WIN_ROWS - 1)

    def one_row(args):
        q_row, rs, dr = args
        k_rows = lax.dynamic_slice_in_dim(kg, rs, kr, axis=1)
        v_rows = lax.dynamic_slice_in_dim(vg, rs, kr, axis=1)
        k_win = k_rows[:, :, col_idx]
        v_win = v_rows[:, :, col_idx]
        bias = rpb[:, dr][:, :, dc_idx].transpose(0, 2, 1, 3)
        s_loc = (jnp.einsum('bqhd,brqchd->bhqrc', q_row, k_win).astype(jnp.float32) * scale
                 + bias[None].astype(jnp.float32))
        s_ctx = jnp.einsum('bqhd,bkhd->bhqk', q_row, k_ctx).astype(jnp.float32) * scale
        sc = jnp.concatenate([s_loc.reshape(b, h, GRID_W, n_loc), s_ctx], axis=-1)
        p = jax.nn.softmax(sc, axis=-1).astype(v.dtype)
        p_loc = p[..., :n_loc].reshape(b, h, GRID_W, kr, kc)
        p_ctx = p[..., n_loc:]
        return (jnp.einsum('bhqrc,brqchd->bqhd', p_loc, v_win)
                + jnp.einsum('bhqk,bkhd->bqhd', p_ctx, v_ctx))

    out = lax.map(one_row, (qg.transpose(1, 0, 2, 3, 4), row_start, dr_idx))
    return out.transpose(1, 0, 2, 3, 4).reshape(b, s, h * dh)

def context_attention(q, k, v):
    b, n, h, dh = q.shape
    s = jnp.einsum('bqhd,bkhd->bhqk', q, k).astype(jnp.float32) * dh ** -0.5
    p = jax.nn.softmax(s, axis=-1).astype(v.dtype)
    return jnp.einsum('bhqk,bkhd->bqhd', p, v).reshape(b, n, h * dh)

def gated_merge(h, y_four, y_attn, w_gate, w_fo, w_ao, w_o):
    gates = jax.nn.sigmoid(h @ w_gate)
    g_f, g_a = jnp.split(gates, N_BRANCHES, axis=-1)
    merged = g_f * (y_four @ w_fo) + g_a * (y_attn @ w_ao)
    return merged @ w_o

def sqrelu_mlp(h, w1, w2):
    a = jax.nn.relu(h @ w1)
    return (a * a) @ w2

def second_inputs(seed: int = 0) -> dict:
    key = jax.random.key(seed)
    ks = jax.random.split(key, 20)
    nrm = lambda k, shape, s: jax.random.normal(k, shape, jnp.float32) * s
    return {
        "x": nrm(ks[0], (BATCH, SEQ, D_MODEL), 1.0),
        "c": nrm(ks[1], (BATCH, D_MODEL), 1.0),
        "ctx": nrm(ks[2], (BATCH, CTX_LEN, D_MODEL), 1.0),
        "c_ctx": nrm(ks[3], (D_MODEL,), 1.0),
        "w_ada": nrm(ks[4], (DEPTH, D_MODEL, N_MOD * D_MODEL), D_MODEL ** -0.5),
        "b_ada": nrm(ks[5], (DEPTH, N_MOD * D_MODEL), 0.02),
        "norm1_g": 1.0 + nrm(ks[6], (DEPTH, D_MODEL), 0.02),
        "norm2_g": 1.0 + nrm(ks[7], (DEPTH, D_MODEL), 0.02),
        "w_in": nrm(ks[8], (DEPTH, D_MODEL, IN_WIDTH), D_MODEL ** -0.5),
        "q_norm_g": 1.0 + nrm(ks[9], (DEPTH, HEAD_DIM), 0.02),
        "k_norm_g": 1.0 + nrm(ks[10], (DEPTH, HEAD_DIM), 0.02),
        "rpb": nrm(ks[11], (DEPTH, NA_HEADS, 2 * WIN_ROWS - 1, 2 * WIN_COLS - 1), 0.1),
        "w_branch_gate": nrm(ks[12], (DEPTH, D_MODEL, N_BRANCHES * D_MODEL), D_MODEL ** -0.5),
        "w_fourier_out": nrm(ks[13], (DEPTH, FOURIER_WIDTH, D_MODEL), FOURIER_WIDTH ** -0.5),
        "w_attn_out": nrm(ks[14], (DEPTH, NA_WIDTH, D_MODEL), NA_WIDTH ** -0.5),
        "w_out": nrm(ks[15], (DEPTH, D_MODEL, D_MODEL), D_MODEL ** -0.5),
        "w_mlp1": nrm(ks[16], (DEPTH, D_MODEL, D_FF_2), D_MODEL ** -0.5),
        "w_mlp2": nrm(ks[17], (DEPTH, D_FF_2, D_MODEL), D_FF_2 ** -0.5),
    }

def second_block(x, c, ctx, c_ctx, w_ada, b_ada, norm1_g, norm2_g, w_in, q_norm_g, k_norm_g,
              rpb, w_branch_gate, w_fourier_out, w_attn_out, w_out, w_mlp1, w_mlp2):
    h_ctx = ctx
    for l in range(DEPTH):
        last = l == DEPTH - 1
        sh1, sc1, g1, sh2, sc2, g2 = [m[:, None, :] for m in ada_mod(c, w_ada[l], b_ada[l])]
        csh1, csc1, cg1, csh2, csc2, cg2 = ada_mod(c_ctx, w_ada[l], b_ada[l])

        hc = modulate(rms_norm_2(h_ctx, norm1_g[l]), csh1, csc1)
        fc, qc, kc, vc = split_projection(hc @ w_in[l])
        kc = rms_norm_2(kc, k_norm_g[l])

        hx = modulate(rms_norm_2(x, norm1_g[l]), sh1, sc1)
        fx, qx, kx, vx = split_projection(hx @ w_in[l])
        qx = axial_rope(rms_norm_2(qx, q_norm_g[l]))
        kx = axial_rope(rms_norm_2(kx, k_norm_g[l]))
        y_four = fourier_mix(fx)
        y_attn = neighbourhood_attention(qx, kx, vx, kc, vc, rpb[l])
        mixed = gated_merge(hx, y_four, y_attn, w_branch_gate[l], w_fourier_out[l],
                            w_attn_out[l], w_out[l])
        x = x + g1 * mixed
        hx2 = modulate(rms_norm_2(x, norm2_g[l]), sh2, sc2)
        x = x + g2 * sqrelu_mlp(hx2, w_mlp1[l], w_mlp2[l])

        if not last:
            qc = rms_norm_2(qc, q_norm_g[l])
            yc_four = fourier_mix(fc)
            yc_attn = context_attention(qc, kc, vc)
            mixed_c = gated_merge(hc, yc_four, yc_attn, w_branch_gate[l], w_fourier_out[l],
                                  w_attn_out[l], w_out[l])
            h_ctx = h_ctx + cg1 * mixed_c
            hc2 = modulate(rms_norm_2(h_ctx, norm2_g[l]), csh2, csc2)
            h_ctx = h_ctx + cg2 * sqrelu_mlp(hc2, w_mlp1[l], w_mlp2[l])
    return x


def setup_inputs(seed=0):
    out = dict(first_inputs(seed))
    for name, value in second_inputs(seed + 1).items():
        if name != "x":
            out[name + "_2"] = value
    return out


def reference(
    x, pre_mix_norm, w_in, gdn_conv_w, gdn_a_log, gdn_dt_bias, gdn_norm_w, ssd_conv_w,
    ssd_conv_b, ssd_a_log, ssd_dt_bias, ssd_d, ssd_norm_w, w_out, post_mix_norm, pre_ffn_norm,
    w_up, ffn_conv_w, ffn_conv_b, w_down, post_ffn_norm, c_2, ctx_2, c_ctx_2, w_ada_2, b_ada_2,
    norm1_g_2, norm2_g_2, w_in_2, q_norm_g_2, k_norm_g_2, rpb_2, w_branch_gate_2,
    w_fourier_out_2, w_attn_out_2, w_out_2, w_mlp1_2, w_mlp2_2,
):
    x = first_block(
        x, pre_mix_norm, w_in, gdn_conv_w, gdn_a_log, gdn_dt_bias, gdn_norm_w, ssd_conv_w,
        ssd_conv_b, ssd_a_log, ssd_dt_bias, ssd_d, ssd_norm_w, w_out, post_mix_norm,
        pre_ffn_norm, w_up, ffn_conv_w, ffn_conv_b, w_down, post_ffn_norm,
    )
    return second_block(
        x, c_2, ctx_2, c_ctx_2, w_ada_2, b_ada_2, norm1_g_2, norm2_g_2, w_in_2, q_norm_g_2,
        k_norm_g_2, rpb_2, w_branch_gate_2, w_fourier_out_2, w_attn_out_2, w_out_2, w_mlp1_2,
        w_mlp2_2,
    )


_drawn_inputs = setup_inputs


def setup_inputs(seed=0):
    import zlib

    import numpy as np

    out = dict(_drawn_inputs(seed))
    spreads = {}
    factors = {'ssd_conv_b': 2.96,
     'ffn_conv_b': 3.436,
     'ctx_2': 4.15,
     'norm1_g_2': 8.0,
     'norm2_g_2': 12.384,
     'q_norm_g_2': 8.0,
     'k_norm_g_2': 8.0,
     'rpb_2': 8.0}
    for name, (base, spread) in spreads.items():
        noise = np.random.default_rng([zlib.crc32(name.encode()), seed]).standard_normal(out[name].shape)
        drawn = base * np.exp(spread * noise) if base else spread * noise
        out[name] = __import__('jax').numpy.asarray(drawn.astype(out[name].dtype))
    for name, factor in factors.items():
        out[name] = (out[name] * factor).astype(out[name].dtype)
    return out
```

```python
from contextlib import ExitStack

import concourse.bass as bass
import numpy as np
from concourse import mybir

F32 = mybir.dt.float32
F32R = mybir.dt.float32r
U32 = mybir.dt.uint32
ACT = mybir.ActivationFunctionType
ALU = mybir.AluOpType
AX = mybir.AxisListType
ds = bass.ds

P = 128
T = 512
NT = T // P
D = 1024
KD = D // P
H = 8
HS = 16
PD = 64
CH = 36
Q0, K0, V0, X0, B0, C0 = 0, 8, 16, 24, 32, 34
FF = 22
MF = 32
NADA = 48
EPS = 1e-6
LEVELS = 7
NEG = -1e30
GRID = 64
AH_ = 8
DH = 64
CTX = 256
NKEY = T + CTX

CONV_N = 0
Z_N = CONV_N + CH
WO_N = Z_N + 16
UP_N = WO_N + 16
DN_N = UP_N + 2 * FF + NADA
PR_N = DN_N + FF
GT_N = PR_N + 16
FA_N = GT_N + 16
W2_N = FA_N + 8
M1_N = W2_N + 8
M2_N = M1_N + MF
END_N = M2_N + MF
WO_A, DN_A, W2_A, M2_A = 0, 16, 16 + FF, 24 + FF


def constants():
    i = np.arange(P)
    ident = np.eye(P)
    upper = (i[:, None] <= i[None, :]).astype(np.float64)
    cols = [ident, upper, np.ones((P, P)), np.where(upper > 0, 0.0, NEG)]
    for level in range(LEVELS):
        s = 1 << level
        pair = (i[:, None] // (2 * s) == i[None, :] // (2 * s))
        low = pair & (i[:, None] % (2 * s) >= s) & (i[None, :] % (2 * s) < s)
        cols += [low.astype(np.float64), low.T.astype(np.float64)]
    cc = GRID - 1 - i % GRID
    start = np.clip(cc - 8, 0, GRID - 16)
    c = np.arange(GRID)
    cols.append(np.where((c[None] >= start[:, None]) & (c[None] < start[:, None] + 16), 0.0, NEG))
    ang = 2 * np.pi * np.outer(i, i) / P
    cols += [np.cos(ang), np.sin(ang)]
    inv = 10000.0 ** (-np.arange(0, 32, 2, dtype=np.float64) / 32)
    for fn in (np.cos, np.sin):
        for t in range(NT):
            tok = t * P + i
            a = np.stack([np.outer(tok // GRID, inv), np.outer(tok % GRID, inv)], 1)
            cols.append(fn(a).reshape(P, 32))
    flip = (i[:, None] // GRID == i[None, :] // GRID) & ((i[:, None] + i[None, :]) % GRID == GRID - 1)
    cols.append(flip.astype(np.float64))
    return np.concatenate(cols, 1).astype(np.float32)


def transforms():
    i = np.arange(T)
    ang = 2 * np.pi * (np.outer(i, i) % T) / T
    scale = (T * P) ** -0.5
    return np.stack([np.cos(ang) * scale, -np.sin(ang) * scale]).astype(np.float32)


IDENT, UPPER, ONES, NEGM, LEVEL = 0, P, 2 * P, 3 * P, 4 * P
COLMASK = LEVEL + 2 * LEVELS * P
DFT = COLMASK + GRID
COS = DFT + 2 * P
SIN = COS + NT * 32
FLIP = SIN + NT * 32
NCST = FLIP + P

FT_ = 0
X1_ = 0
FF_ = 4096
MR_ = 15360
M_ = CH * T
XN_ = M_
STG_ = M_ + 4096
LVL_ = STG_ + 640
CT_ = LVL_ + 1792
HT_ = CT_ + 1024
WB_ = M_ + 4096
YT_ = WB_ + 1024
F_, QK_, V_ = 4096, 6144, 11264
R1_ = 14336
QT_, KT_, C2_ = 22528, 24576, 27648
MT_ = 6144
M1_ = 4096
ARENA = 28800
QE_, R_, TT_, NM_, PP_, NW_, VN_, SD_, SS_ = (M_ + 1024 * i for i in range(9))
AP_, AG_, APT_ = QK_, R1_, R1_ + 2048
BANKS = [[(4, 0), (5, 0), (6, 0), (7, 0)],
         [(0, 1), (1, 2), (2, 3), (3, 4), (4, 5), (5, 6)],
         [(6, 7), (7, 8), (0, 9), (1, 10), (2, 11), (3, 12)]]
STAGED = [96, 77, 96, 88, 80]
CONSTS, PARAMS = 2, 22
JK_ = 4096
QS_ = 28224


def program(nc, a, cst, dft, gmod, gpad, out):
    ctx = ExitStack()
    with ctx:
        def sb(name, shape, dt=F32):
            return ctx.enter_context(nc.sbuf_tensor(name, shape, dt))

        S = {}

        def sem(name):
            if name not in S:
                S[name] = ctx.enter_context(nc.semaphore(name))
            return S[name]

        WH = sb("w_high", [P, 2, 1024], F32R)
        WL = sb("w_low", [P, 2, 1024], F32R)
        AH = sb("act_high", [P, 4, 512], F32R)
        AL = sb("act_low", [P, 4, 512], F32R)
        HH = sb("h_high", [P, KD, T], F32R)
        HL = sb("h_low", [P, KD, T], F32R)
        SH = sb("small_w_high", [P, KD, 32], F32R)
        SL = sb("small_w_low", [P, KD, 32], F32R)
        CD4 = sb("cond_parts", [P, KD, 4], F32R)
        RAW = sb("w_raw", [P, 4, 1024])
        C1 = sb("masks", [P, 512])
        LV = sb("level_masks", [P, 2 * LEVELS, P], mybir.dt.uint8)
        PAR = sb("params", [P, 5, P])
        CW = sb("conv_params", [P, 5 * CH])
        A = sb("arena", [P, ARENA])
        PS = ctx.enter_context(nc.psum_tensor("acc", [P, 8, 512], F32))
        PSF = PS[:, :, :].rearrange("p a b -> p (a b)")
        small_at = [0]
        SM = sb("small", [P, 1600])

        def small(*shape):
            n = int(np.prod(shape))
            v = SM[:, small_at[0]:small_at[0] + n]
            small_at[0] += n
            assert small_at[0] <= 1600
            if len(shape) == 2:
                return v.rearrange("p (a b) -> p a b", b=shape[1])
            if len(shape) == 3:
                return v.rearrange("p (a b c) -> p a b c", b=shape[1], c=shape[2])
            return v

        def arena(at, *shape):
            v = A[:, at:at + int(np.prod(shape))]
            if len(shape) == 2:
                return v.rearrange("p (a b) -> p a b", b=shape[1])
            if len(shape) == 3:
                return v.rearrange("p (a b c) -> p a b c", b=shape[1], c=shape[2])
            return v

        IDN, UPR, ONE, NGM = (C1[:, k * P:(k + 1) * P] for k in range(4))
        FLP = UPR
        FT = arena(FT_, CH, T)
        XN = arena(XN_, NT, D)
        STG = arena(STG_, 5, P)
        LVF = arena(LVL_, 2 * LEVELS * P)
        CT = arena(CT_, 2, T)
        HT = arena(HT_, 2, T)
        WB = arena(WB_, D)
        YT = arena(YT_, D)
        X1 = arena(X1_, NT, D)
        FFT = arena(FF_, FF, T)
        MR = A[0:4, MR_:MR_ + 6 * D]

        sumsq = small(18)
        meansq = small(18)
        rstd = small(18)
        half = small(64)
        small_w = arena(HT_ + 1024, KD, 32)
        head_bias = small(24)
        head_log = small(24)
        skip_d = small(HS)
        modT = small(NADA, 2)
        affine = small(3, KD)
        cond = small(KD, 2)
        proj = arena(HT_ + 1280, NT, 32)
        sp_x, sp_e, sp_s, sp_q = (arena(SS_ + 96 * i, NT, 24) for i in range(4))
        soft = small(NT, 24)
        nega = small(24)
        logdec = small(NT, 24)
        ncum = small(NT, 24)
        qkg = SM[:, small_at[0]:small_at[0] + 2 * DH]
        ecum = small(NT, 24)
        edec = small(NT, 24)
        etot = small(NT, 24)
        beta = small(NT, H)
        join = SM[0:4, small_at[0]:small_at[0] + 2]
        small_at[0] += 2
        qks = small(NT, 16)
        qkr = small(NT, 16)
        nrk = small(NT, H)
        brk = small(NT, H)
        kbs = small(NT, H)
        kds = small(NT, H)
        rq2 = small(NT, H)
        oss = small(NT, H)
        ors = small(NT, H)
        qkss = small(10, AH_)
        qkrs = small(10, AH_)
        smax = small(AH_ * NT)
        sumsq2 = small(8)
        meansq2 = small(8)
        rstd2 = small(8)
        eps_col = small(1)
        GT_T = arena(YT_, T)
        ssum = small(AH_ * NT)
        srec = small(AH_ * NT)

        w_in = a["w_in"][0]
        w_in_v = w_in.rearrange("(k p) n -> p k n", p=P)
        w_up_v = a["w_up"][0].rearrange("(k p) n -> p k n", p=P)
        w_in2_v = a["w_in_2"][0].rearrange("(k p) n -> p k n", p=P)
        gate_v = a["w_branch_gate_2"][0].rearrange("(k p) n -> p k n", p=P)
        fo_v = a["w_fourier_out_2"][0].rearrange("(k p) n -> p k n", p=P)
        ao_v = a["w_attn_out_2"][0].rearrange("(k p) n -> p k n", p=P)
        mlp1_v = a["w_mlp1_2"][0].rearrange("(k p) n -> p k n", p=P)
        x_rows = a["x"][0].rearrange("(t p) d -> t p d", p=P)
        ctx_rows = a["ctx_2"][0].rearrange("(t p) d -> t p d", p=P)
        out_rows = out[0].rearrange("(t p) d -> t p d", p=P)

        def blocks(eng, n, body, whole=0):
            full = n // 4 - whole
            if full > 1:
                with eng.Fori(0, full) as g:
                    for j in range(4):
                        body(g, j)
            else:
                full = 0
            for g in range(full, (n + 3) // 4):
                for j in range(min(4, n - 4 * g)):
                    body(g, j)

        def up_groups(eng, body):
            with eng.Fori(0, FF // 4) as cg:
                for i in range(4):
                    for j in range(4):
                        body(4 * cg + i, i, j, cg)
            for i in range(FF % 4):
                for j in range(4):
                    body(FF // 4 * 4 + i, i, j, FF // 4)

        def parts(n):
            if n % 4 < 2:
                return [WH[:, n % 2, :], WL[:, n % 2, :]]
            r = slice(2 * (n % 2), 2 * (n % 2) + 2)
            return [v[:, r, :].rearrange("p a b -> p (a b)") for v in (AH, AL)]

        def probs(i):
            return arena(AP_ + (i % 2) * NKEY, NKEY)

        def probs_t(h):
            return arena(APT_ + (h % 2) * 6 * T, 6, T)

        def turned(i):
            b = i % 2
            return PS[:, 4 + 2 * b, :], PS[:, 5, b * CTX:(b + 1) * CTX]

        block = ctx.enter_context(nc.Block())

        def up_to(v, n):
            return v.unsqueeze(2).to_broadcast([P, n, P])

        def each(v, n):
            return v.unsqueeze(1).to_broadcast([P, n, v.shape[1]])

        @block.sync
        def _(sp):
            for t in range(NT):
                sp.dma_start(XN[:, t, :], x_rows[t]).then_inc(sem(f"x_in{t}"), 16)

            def load(g, off, src, shape):
                sp.wait_ge(sem("w_low"), 4 * g + off + 1)
                dst = RAW[:, off % 4, :]
                if shape is not None:
                    dst = dst.rearrange("p (k c) -> p k c", c=shape)
                sp.dma_start(dst, src).then_inc(sem(f"w_in{off % 4}"), 16)

            def columns(n0, first, view, w=P, step=1):
                def body(g, j):
                    load(g, n0 + j, view[:, :, ds(first + g * (4 * w) + j * w, w)], w)
                return body

            def rows(n0, view):
                v = view.rearrange("(k p) n -> k p n", p=P)

                def body(g, j):
                    load(g, n0 + j, v[4 * g + j], None)
                return body

            blocks(sp, X0, columns(CONV_N, 0, w_in_v))
            blocks(sp, CH - X0, columns(CONV_N + X0, 5136, w_in_v))
            blocks(sp, 8, columns(Z_N, 4112, w_in_v))
            blocks(sp, 8, columns(Z_N + 8, 3072, w_in_v))
            blocks(sp, 16, rows(WO_N, a["w_out"][0]))

            ada_rows = a["w_ada_2"][0]

            def up(q, i, j, cg):
                if j < 2:
                    load(q, UP_N + j, w_up_v[:, :, ds(q * P + j * (FF * P), P)], P)
                else:
                    k = 2 * i + j - 2
                    load(q, UP_N + j, ada_rows[k * P:(k + 1) * P, ds(cg * D, D)], None)

            up_groups(sp, up)
            for j in range(4):
                load(0, UP_N + 4 * FF + j, ada_rows[(4 + j) * P:(5 + j) * P, 5 * D:6 * D], None)
            blocks(sp, FF, rows(DN_N, a["w_down"][0]))
            blocks(sp, 4, columns(PR_N, 0, w_in2_v))
            for part in range(3):
                for j in range(4):
                    load(0, PR_N + 4 + 4 * part + j,
                         w_in2_v[:, 2 * j:2 * j + 2, 512 * (part + 1):512 * (part + 2)], 512)
            blocks(sp, 16, columns(GT_N, 0, gate_v))
            for b in range(4):
                load(0, FA_N + 2 * b, fo_v[:, :, 256 * b:256 * (b + 1)], 256)
                load(0, FA_N + 2 * b + 1, ao_v[:, :, 256 * b:256 * (b + 1)], 256)
            blocks(sp, 8, rows(W2_N, a["w_out_2"][0]))
            blocks(sp, MF, columns(M1_N, 0, mlp1_v))
            blocks(sp, MF, rows(M2_N, a["w_mlp2_2"][0]))
            for t in range(NT):
                sp.wait_ge(sem("x_res"), 3 * NT + t + 1)
                sp.dma_start(out_rows[t], X1[:, t, :]).then_inc(sem("stored"), 16)
            sp.wait_ge(sem("stored"), 16 * NT)

        @block.tensor
        def _(pe):
            def products(out_, wh, wl, xh, xl, start, stop):
                pe.matmul(out_, wh, xh, start=start, stop=False)
                pe.matmul(out_, wh, xl, start=False, stop=False)
                return pe.matmul(out_, wl, xh, start=False, stop=stop)

            def split_ready(g, off):
                pe.wait_ge(sem("w_low"), 4 * g + off + 1 + 4)

            def column_block(g, off, bank, xh, xl, n=T, first=None):
                split_ready(g, off)
                s = off % 2
                for k in range(KD):
                    if first is not None:
                        pe.wait_ge(sem("n_low"), first + k + 1)
                    c = slice(k * P, (k + 1) * P)
                    m = products(PS[:, bank, 0:n], WH[:, s, c], WL[:, s, c], xh[:, k, :], xl[:, k, :],
                                 k == 0, k == KD - 1)
                m.then_inc(sem("w_used"), 1)

            def row_block(g, off, j, a0, k_is_0, k_is_last):
                split_ready(g, off)
                pe.wait_ge(sem("a_low"), a0 + 4 * g + j + 1)
                s, r = off % 2, (a0 + j) % 4
                for t in range(NT):
                    tc = slice(t * P, (t + 1) * P)
                    for f in range(2):
                        fc = slice(f * 512, (f + 1) * 512)
                        o = PS[:, 2 * t + f, :]
                        pe.matmul(o, AH[:, r, tc], WH[:, s, fc], start=k_is_0, stop=False)
                        pe.matmul(o, AH[:, r, tc], WL[:, s, fc], start=False, stop=False)
                        m = pe.matmul(o, AL[:, r, tc], WH[:, s, fc], start=False, stop=k_is_last)
                m.then_inc(sem("w_used"), 1)

            def down(n0, a0, n):
                def body(g, j, first=False, last=False):
                    row_block(g, n0 + j, j, a0, first and j == 0, last)
                for j in range(4):
                    body(0, j, first=True)
                full = n // 4
                mid_end = full if n % 4 else full - 1
                if mid_end > 2:
                    with pe.Fori(1, mid_end) as g:
                        for j in range(4):
                            body(g, j)
                else:
                    for g in range(1, mid_end):
                        for j in range(4):
                            body(g, j)
                for g in range(mid_end, (n + 3) // 4):
                    for j in range(min(4, n - 4 * g)):
                        body(g, j, last=4 * g + j == n - 1)

            def turn(job, x, nt, tiles):
                pe.wait_ge(sem("n_x"), tiles + nt)
                for k in range(KD):
                    if 8 * job + k > 3:
                        pe.wait_ge(sem("n_low"), 8 * job + k - 3)
                    for t in range(nt):
                        m = pe.transpose(PS[:, 4 + k % 4, t * P:(t + 1) * P],
                                         x[:, t, k * P:(k + 1) * P], IDN)
                    m.then_inc(sem("n_turned"), 1)

            pe.wait_ge(sem("consts_in"), CONSTS * 16)
            pe.wait_ge(sem("params_in"), PARAMS * 16)
            for s, r in enumerate(STAGED):
                m = pe.transpose(PS[:, s // 4, (s % 4) * P:(s % 4) * P + r], STG[0:r, s, :],
                                 IDN[0:r, 0:r])
            m.then_inc(sem("params_turned"), 1)
            turn(0, XN, NT, 0)
            pe.wait_ge(sem("params_out"), 5)

            def conv(g, j):
                pe.wait_ge(sem("conv_step"), 3 * (4 * g + j) + 3)
                column_block(g, CONV_N + j, j, HH, HL,
                             first=0 if isinstance(g, int) and g == 0 else None)

            for j in range(4):
                conv(0, j)
            with pe.Fori(1, CH // 4) as g:
                for j in range(4):
                    conv(g, j)
            pe.wait_ge(sem("small_low"), 1)
            for t in range(NT):
                for k in range(KD):
                    tc = slice(t * P, (t + 1) * P)
                    o = PS[:, 7, t * 32:(t + 1) * 32]
                    pe.matmul(o, HH[:, k, tc], SH[:, k, :], start=k == 0, stop=False)
                    pe.matmul(o, HH[:, k, tc], SL[:, k, :], start=False, stop=False)
                    m = pe.matmul(o, HL[:, k, tc], SH[:, k, :], start=False, stop=k == KD - 1)
            m.then_inc(sem("proj_done"), 1)
            for i in range(16):
                pe.wait_ge(sem("qk_square"), i + 1)
                for c in range(NT):
                    o = 2 * (c * 16 + i)
                    m = pe.matmul(PS[:, 6, o:o + 2], arena(QE_ + (i % 4) * T, T)[:, c * P:(c + 1) * P],
                                  ONE[:, 0:2], start=True, stop=True)
                m.then_inc(sem("qk_sum"), 1)
            pe.wait_ge(sem("logdec_ready"), 1)
            pe.matmul(PS[:, 4, 0:96], UPR, logdec.rearrange("p a b -> p (a b)"), start=True, stop=True)
            pe.matmul(PS[:, 5, 0:96], ONE, logdec.rearrange("p a b -> p (a b)"), start=True, stop=True)\
                .then_inc(sem("cum_done"), 1)
            pe.wait_ge(sem("scales_ready"), 1)

            def four(q):
                return range(4 * q, 4 * q + 4)

            for c in range(NT):
                tc = slice(c * P, (c + 1) * P)

                def tile(at, h):
                    return arena(at + h * P, P)

                if c:
                    pe.wait_ge(sem("y_turned_out"), 2 * c)
                for q in range(2):
                    for h in four(q):
                        m = pe.matmul(PS[:, q, (h % 4) * P:(h % 4 + 1) * P],
                                      logdec[:, c, h:h + 1].to_broadcast([P, P]), UPR,
                                      start=True, stop=True)
                    m.then_inc(sem("d_cum"), 1)
                for q in range(2):
                    for h in four(q):
                        pe.matmul(PS[:, 2 + q, (h % 4) * P:(h % 4 + 1) * P],
                                  brk[:, c, h:h + 1].to_broadcast([P, P]), IDN, start=True, stop=True)
                    for h in four(q):
                        pe.matmul(PS[:, 4 + q, (h % 4) * P:(h % 4 + 1) * P], FT[:, K0 + h, tc],
                                  FT[:, K0 + h, tc], start=True, stop=True)
                    for h in four(q):
                        m = pe.matmul(PS[:, 6 + q, (h % 4) * P:(h % 4 + 1) * P], FT[:, K0 + h, tc],
                                      FT[:, Q0 + h, tc], start=True, stop=True)
                    m.then_inc(sem("d_gram"), 1)
                for q in range(2):
                    pe.wait_ge(sem("d_r0"), 2 * c + q + 1)
                    for h in four(q):
                        m = pe.transpose(PS[:, q, (h % 4) * P:(h % 4 + 1) * P], tile(R_, h), IDN)
                    m.then_inc(sem("d_r0_turned"), 1)
                for level in range(1, LEVELS):
                    u = 2 * (c * (LEVELS - 1) + level - 1) + 1
                    for q in range(2):
                        pe.wait_ge(sem("d_level"), 2 * (c * LEVELS + level - 1) + q + 1)
                        for h in four(q):
                            m = pe.matmul(PS[:, 2 + q, (h % 4) * P:(h % 4 + 1) * P], tile(NM_, h),
                                          tile(TT_, h), start=True, stop=True)
                        m.then_inc(sem("d_nt"), 1)
                    for q in range(2):
                        pe.wait_ge(sem("d_nt_out"), u + q)
                        if level < LEVELS - 1:
                            for h in four(q):
                                pe.matmul(PS[:, 4 + q, (h % 4) * P:(h % 4 + 1) * P], tile(R_, h),
                                          tile(PP_, h), start=True, stop=True)
                        for h in four(q):
                            m = pe.matmul(PS[:, 6 + q, (h % 4) * P:(h % 4 + 1) * P], tile(PP_, h),
                                          tile(R_, h), start=True, stop=True)
                        m.then_inc(sem("d_tnt"), 1)
                for q in range(2):
                    for h in four(q):
                        pe.transpose(PS[:, q, (h % 4) * P:(h % 4 + 1) * P], FT[:, K0 + h, tc], IDN)
                    for h in four(q):
                        m = pe.transpose(PS[:, 2 + q, (h % 4) * P:(h % 4 + 1) * P], FT[:, V0 + h, tc], IDN)
                    m.then_inc(sem("d_kv_turned"), 1)
                for q in range(2):
                    pe.wait_ge(sem("d_kv_out"), 2 * c + q + 1)
                    for h in four(q):
                        m = pe.matmul(PS[:, 4 + q, (h % 4) * P:(h % 4 + 1) * P], tile(TT_, h),
                                      tile(R_, h), start=True, stop=True)
                    m.then_inc(sem("d_w"), 1)
                for q in range(2):
                    pe.wait_ge(sem("d_w_out"), 2 * c + q + 1)
                    for h in four(q):
                        o = PS[:, 6 + q, (h % 4) * P:(h % 4 + 1) * P]
                        m = pe.matmul(o, tile(R_, h), tile(PP_, h), start=True, stop=c == 0)
                        if c:
                            m = pe.matmul(o, tile(NW_, h), tile(SD_, h), start=False, stop=True)
                    m.then_inc(sem("d_new"), 1)
                    if c:
                        for h in four(q):
                            m = pe.matmul(PS[:, q, (h % 4) * P:(h % 4 + 1) * P], FT[:, Q0 + h, tc],
                                          tile(SD_, h), start=True, stop=True)
                        m.then_inc(sem("d_qs"), 1)
                for q in range(2):
                    pe.wait_ge(sem("d_new_out"), 2 * c + q + 1)
                    for h in four(q):
                        pe.matmul(PS[:, 2 + q, (h % 4) * P:(h % 4 + 1) * P], tile(QE_, h),
                                  tile(VN_, h), start=True, stop=True)
                    for h in four(q):
                        m = pe.matmul(PS[:, 4 + q, (h % 4) * P:(h % 4 + 1) * P], tile(NM_, h),
                                      tile(VN_, h), start=True, stop=True)
                    m.then_inc(sem("d_out"), 1)
                for q in range(2):
                    pe.wait_ge(sem("d_normed"), 2 * c + q + 1)
                    for h in four(q):
                        m = pe.transpose(PS[:, 6 + q, (h % 4) * P:(h % 4 + 1) * P], tile(R_, h), IDN)
                    m.then_inc(sem("d_o_turned"), 1)
                pe.wait_ge(sem("d_state"), 2 * c + 2)
                for i in range(8):
                    m = pe.transpose(PS[:, i // 4, (i % 4) * P:(i % 4 + 1) * P], FT[:, X0 + i, tc], IDN)
                for g in range(2):
                    m = pe.transpose(PS[:, 2, g * P:(g + 1) * P], FT[:, B0 + g, tc], IDN)
                m.then_inc(sem("s_turned"), 1)
                for g in range(2):
                    m = pe.matmul(PS[:, 3, g * P:(g + 1) * P], FT[:, B0 + g, tc], FT[:, C0 + g, tc],
                                  start=True, stop=True)
                for g in range(2):
                    if g:
                        pe.wait_ge(sem("s_arg"), 2 * c + g)
                    for h in range(8):
                        m = pe.matmul(PS[:, 4 + h // 4, (h % 4) * P:(h % 4 + 1) * P],
                                      logdec[:, c, 8 + 8 * g + h:9 + 8 * g + h].to_broadcast([P, P]),
                                      UPR, start=True, stop=True)
                    m.then_inc(sem("s_cum"), 1)
                    pe.wait_ge(sem("s_m"), 2 * c + g + 1)
                    if g or c:
                        pe.wait_ge(sem("s_y"), 2 * c + g)
                    if g == 0:
                        pe.wait_ge(sem("d_o_out"), 2 * c + 2)
                    for h in range(8):
                        m = pe.matmul(PS[:, 6, h * PD:(h + 1) * PD], tile(R_, h),
                                      arena(TT_ + (8 * g + h) * PD, PD), start=True, stop=True)
                    if c:
                        m = pe.matmul(PS[:, 7, :], FT[:, C0 + g, tc], arena(SS_ + g * 512, 512),
                                      start=True, stop=True)
                    m = pe.matmul(PS[:, 2, :], arena(NW_ + g * P, P), arena(NM_ + g * 512, 512),
                                  start=True, stop=True)
                    m.then_inc(sem("s_sum"), 1)
                    pe.wait_ge(sem("s_y"), 2 * c + g + 1)
                    for i in range(4):
                        m = pe.transpose(PS[:, g, i * P:(i + 1) * P],
                                         arena(VN_ + g * 512 + i * P, P), IDN)
                    m.then_inc(sem("y_turned"), 1)
            pe.wait_ge(sem("y_turned_out"), 2 * NT)

            def gated(g, j):
                pe.wait_ge(sem("z_step"), 4 * g + j + 1)
                column_block(g, Z_N + j, j, HH, HL)

            blocks(pe, 16, gated)
            for g in range(2):
                for i in range(4):
                    pe.wait_ge(sem("y_square"), 4 * g + i + 1)
                    m = pe.matmul(PS[:, 4 + g, :], ONE, arena(NM_ + (4 * g + i) * T, T),
                                  start=i == 0, stop=i == 3)
                    m.then_inc(sem("y_sum"), 1)
            pe.wait_ge(sem("y_norm"), 8)
            down(WO_N, WO_A, 16)
            turn(1, XN, NT, 4)

            def modulation(q, j, k):
                split_ready(q, UP_N + j)
                wh, wl = parts(j)
                for v in range(2):
                    vc = slice(v * 512, (v + 1) * 512)
                    pe.matmul(PS[0:4, 4 + v, :], CD4[:, k, :], wh[:, vc], start=k == 0, stop=False)
                    m = pe.matmul(PS[0:4, 4 + v, :], CD4[:, k, :], wl[:, vc], start=False,
                                  stop=k == KD - 1)
                m.then_inc(sem("w_used"), 1)

            def ffn(q, i, j, cg):
                if j < 2:
                    pe.wait_ge(sem("ffn_step"), 5 * q + [2, 4][j])
                    column_block(q, UP_N + j, j, HH, HL)
                else:
                    if i == 0 and j == 2:
                        pe.wait_ge(sem("mod_rows"), cg + 1)
                    modulation(q, j, 2 * i + j - 2)

            pe.wait_ge(sem("n_low"), 16)
            up_groups(pe, ffn)
            for j in range(4):
                modulation(FF, j, 4 + j)
            pe.wait_ge(sem("join_ready"), 1)
            pe.wait_ge(sem("mod_rows"), 7)
            for i in range(NADA):
                m = pe.matmul(PS[:, 6, 2 * i:2 * i + 2], MR[:, i * P:(i + 1) * P], join, start=True, stop=True)
            m.then_inc(sem("mod_turned"), 1)
            pe.wait_ge(sem("mod_out"), 1)
            down(DN_N, DN_A, FF)
            turn(2, XN, NT, 8)
            turn(3, arena(QT_, 2, D), 2, 12)
            for j in range(4):
                column_block(0, PR_N + j, j, HH, HL, first=16 if j == 0 else None)
            pe.wait_ge(sem("n_low"), 32)
            XH = AH[:, :, :].rearrange("p a b -> p (a b)").rearrange("p (k t) -> p k t", t=CTX)
            XL = AL[:, :, :].rearrange("p a b -> p (a b)").rearrange("p (k t) -> p k t", t=CTX)
            for part in range(3):
                for b in range(4):
                    n = PR_N + 4 + 4 * part + b
                    split_ready(0, n)
                    for i in range(4 if part == 0 else 6):
                        bank, free = BANKS[part][i]
                        if b == 0 and free:
                            pe.wait_ge(sem("pr_out"), free)
                        for kk in range(2):
                            k = 2 * b + kk
                            if i < 4:
                                xh, xl = HH[:, k, i * P:(i + 1) * P], HL[:, k, i * P:(i + 1) * P]
                            else:
                                xh, xl = XH[:, k, (i - 4) * P:(i - 3) * P], XL[:, k, (i - 4) * P:(i - 3) * P]
                            wc = slice(kk * 512, (kk + 1) * 512)
                            o = PS[:, bank, :]
                            pe.matmul(o, xh, WH[:, n % 2, wc], start=k == 0, stop=False)
                            pe.matmul(o, xh, WL[:, n % 2, wc], start=False, stop=False)
                            m = pe.matmul(o, xl, WH[:, n % 2, wc], start=False, stop=k == KD - 1)
                    m.then_inc(sem("w_used"), 1)
            CD = arena(C2_ + GRID, 2 * P)
            V12 = arena(R1_, NT, 4, 2 * P)
            CSN = arena(R1_ + 4096, 2, NT, T)
            pe.wait_ge(sem("pr_out"), 20)
            pe.wait_ge(sem("dft_in"), 32)
            for t in range(NT):
                for u in range(2):
                    for gr in range(2 * u, 2 * u + 2):
                        m = pe.matmul(PS[:, 2 * (t % 2) + u, (gr % 2) * 256:(gr % 2 + 1) * 256],
                                      arena(F_ + gr * T + t * P, P), CD, start=True, stop=True)
                    m.then_inc(sem("f_mix"), 1)
                if t:
                    pe.wait_ge(sem("f_mix_out"), 2 * t)
            pe.wait_ge(sem("f_mix_out"), 8)
            for gr in range(4):
                for kt in range(NT):
                    for v in range(2):
                        m = pe.matmul(PS[:, 4 + gr, :], V12[:, kt, gr, v * P:(v + 1) * P],
                                      CSN[:, v, kt, :], start=kt == 0 and v == 0,
                                      stop=kt == NT - 1 and v == 1)
                m.then_inc(sem("f_done"), 1)
            QKt = arena(QK_, 10, 4, P)
            for i in range(10):
                pe.wait_ge(sem("qk_ready"), i + 1)
                if i > 3:
                    pe.wait_ge(sem("qk_turned_out"), i - 3)
                for f in range(4):
                    m = pe.transpose(PS[:, i % 4, f * P:(f + 1) * P], QKt[:, i, f, :], IDN)
                m.then_inc(sem("qk_turned"), 1)
            QT = arena(QT_, 4, T)
            KT = arena(KT_, 4, NKEY)
            V = arena(V_, 6, T)
            pe.wait_ge(sem("qk_turned_out"), 10)
            pe.wait_ge(sem("f_out"), 4)

            def scores(i):
                h, t = divmod(i, NT)
                r = slice(DH * (h % 2), DH * (h % 2) + DH)
                if i > 1:
                    pe.wait_ge(sem("at_exp"), i - 1)
                pe.wait_ge(sem("bias_ready"), h + 1)
                pe.matmul(PS[:, 2 * (i % 2), :], FLP,
                          arena(AG_ + (h % 2) * 1024 + (7 - 2 * t) * GRID, T), start=True, stop=False)
                pe.matmul(PS[:, 2 * (i % 2), :], QT[r, h // 2, t * P:(t + 1) * P], KT[r, h // 2, 0:T],
                          start=False, stop=True)
                pe.matmul(PS[:, 2 * (i % 2) + 1, 0:CTX], QT[r, h // 2, t * P:(t + 1) * P],
                          KT[r, h // 2, T:NKEY], start=True, stop=True).then_inc(sem("at_scores"), 1)

            def values(h):
                pe.wait_ge(sem("at_main_out"), NT * (h + 1))
                pe.wait_ge(sem("at_ctx_out"), NT * (h + 1))
                if h:
                    pe.wait_ge(sem("at_o_out"), h)
                r = slice(DH * (h % 2), DH * (h % 2) + DH)
                for kt in range(6):
                    m = pe.matmul(PS[r, 7, :], V[:, kt, h * DH:(h + 1) * DH], probs_t(h)[:, kt, :],
                                  start=kt == 0, stop=kt == 5)
                m.then_inc(sem("at_o"), 1)

            scores(0)
            for i in range(AH_ * NT):
                if i + 1 < AH_ * NT:
                    scores(i + 1)
                pe.wait_ge(sem("at_scaled"), i + 1)
                if i > 1:
                    pe.wait_ge(sem("at_main_out"), i - 1)
                main, side = turned(i)
                for kt in range(6):
                    if kt == 4 and i:
                        pe.wait_ge(sem("at_ctx_out"), i)
                    o = main[:, kt * P:(kt + 1) * P] if kt < 4 else side[:, (kt - 4) * P:(kt - 3) * P]
                    m = pe.transpose(o, probs(i)[:, kt * P:(kt + 1) * P], IDN)
                m.then_inc(sem("at_p_turned"), 1)
                if i and i % NT == 0:
                    values(i // NT - 1)
            values(AH_ - 1)

            def gate(g, j):
                pe.wait_ge(sem("gate_out"), 4 * g + j + 1)
                column_block(g, GT_N + j, j, HH, HL)

            blocks(pe, 16, gate)
            pe.wait_ge(sem("gate_out"), 20)
            for b in range(4):
                for v in range(2):
                    n = FA_N + 2 * b + v
                    split_ready(0, n)
                    if b == 0:
                        pe.wait_ge(sem("branch_low"), 4 * (v + 1))
                    for mm in range(2):
                        if v == 0 and b:
                            pe.wait_ge(sem("merge_out"), 2 * b + mm - 1)
                        for k in range(4):
                            wc = slice(k * 256 + mm * P, k * 256 + mm * P + P)
                            xh = HH[:, k, :] if v else AH[:, k, :]
                            xl = HL[:, k, :] if v else AL[:, k, :]
                            m = products(PS[:, 2 * mm + v, :], WH[:, n % 2, wc], WL[:, n % 2, wc],
                                         xh, xl, k == 0, k == 3)
                    m.then_inc(sem("w_used"), 1)
            pe.wait_ge(sem("merge_out"), 8)
            down(W2_N, W2_A, 8)
            turn(4, XN, NT, 14)

            def mlp(g, j):
                pe.wait_ge(sem("mlp_out"), 4 * g + j + 1)
                column_block(g, M1_N + j, j, HH, HL,
                             first=32 if isinstance(g, int) and g == 0 and j == 0 else None)

            for j in range(4):
                mlp(0, j)
            with pe.Fori(1, MF // 4) as g:
                for j in range(4):
                    mlp(g, j)
            pe.wait_ge(sem("mlp_out"), MF + 4)
            down(M2_N, M2_A, MF)

        @block.scalar
        def _(act):
            f = act.activation
            act.dma_start(C1[:, :], cst[:, 0:512]).then_inc(sem("consts_in"), 16)
            act.dma_start(LVF, cst[:, LEVEL:COLMASK]).then_inc(sem("consts_in"), 16)

            def par(dst, src):
                act.dma_start(dst, src).then_inc(sem("params_in"), 16)

            def as_rows(name, taps=False):
                v = a[name][0]
                return v.rearrange("k (t p) -> (k t) p", p=P) if taps else v.rearrange("(t p) -> t p", p=P)

            par(STG[0:96, 0, :], as_rows("gdn_conv_w", True))
            par(STG[0:48, 1, :], as_rows("ssd_conv_w", True))
            par(STG[48:60, 1, :], as_rows("ssd_conv_b"))
            par(STG[60:68, 1, :], as_rows("pre_mix_norm"))
            par(STG[68:69, 1, :], as_rows("gdn_norm_w"))
            par(STG[69:77, 1, :], as_rows("ssd_norm_w"))
            par(STG[0:88, 2, :], as_rows("ffn_conv_w", True)[0:88, :])
            par(STG[88:96, 2, :], as_rows("pre_ffn_norm"))
            par(STG[0:44, 3, :], as_rows("ffn_conv_w", True)[88:132, :])
            par(STG[44:88, 3, :], as_rows("ffn_conv_b"))
            par(STG[0:48, 4, :], as_rows("b_ada_2"))
            par(STG[48:56, 4, :], as_rows("norm1_g_2"))
            par(STG[56:64, 4, :], as_rows("norm2_g_2"))
            par(STG[64:72, 4, :], as_rows("c_2"))
            par(STG[72:80, 4, :], a["c_ctx_2"].rearrange("(t p) -> t p", p=P))
            par(small_w[:, :, 0:16], w_in_v[:, :, 4096:4112])
            par(small_w[:, :, 16:32], w_in_v[:, :, 6672:6688])
            par(head_bias[:, 0:8], a["gdn_dt_bias"].to_broadcast([P, 8]))
            par(head_bias[:, 8:24], a["ssd_dt_bias"].to_broadcast([P, HS]))
            par(head_log[:, 0:8], a["gdn_a_log"].to_broadcast([P, 8]))
            par(head_log[:, 8:24], a["ssd_a_log"].to_broadcast([P, HS]))
            par(skip_d, a["ssd_d"].to_broadcast([P, HS]))

            def split(g, off):
                act.wait_ge(sem(f"w_in{off % 4}"), 16 * g + 16 * (off // 4 + 1))
                act.wait_ge(sem("w_used"), 4 * g + off + 1)
                f(WH[:, off % 2, :], RAW[:, off % 4, :], ACT.Copy).then_inc(sem("w_high"), 1)

            def used(g, off):
                act.wait_ge(sem("w_used"), 4 * g + off + 1 + 2)

            def act_split(g, j, a0, n0, src):
                act.wait_ge(sem("w_used"), 4 * g + j + n0 - 4 + 1 + 2)
                f(AH[:, (a0 + j) % 4, :], src[:, 4 * g + j, :], ACT.Copy).then_inc(sem("a_high"), 1)

            def norm(job, x, nt, tiles, ready):
                for t in range(nt):
                    if len(ready) == 2:
                        act.wait_ge(sem(ready[0]), ready[1] + t)
                    else:
                        act.wait_ge(sem(f"{ready[0]}{t}"), 16)
                    junk = arena(JK_, NT, D) if job in (0, 3) else XN
                    f(junk[:, t, :], x[:, t, :], ACT.Square,
                      accum_out=sumsq[:, tiles + t:tiles + t + 1]).then_inc(sem("n_square"), 1)

            def norm_high(job, nt):
                hh = HH if job != 3 else AH[:, :, :].rearrange("p a b -> p (a b)")\
                    .rearrange("p (k t) -> p k t", t=CTX)
                for k in range(KD):
                    act.wait_ge(sem("n_value"), 8 * job + k + 1)
                    f(hh[:, k, :], HT[:, k % 2, 0:nt * P], ACT.Copy).then_inc(sem("n_high"), 1)

            def down(n0, a0, n, src, ready):
                for j in range(2):
                    act.wait_ge(sem(ready[0]), ready[1](j))
                    act_split(0, j, a0, n0, src)

                def body(g, j):
                    if not isinstance(g, int) or 4 * g + j + 2 < n:
                        act.wait_ge(sem(ready[0]), ready[1](4 * g + j + 2))
                        act_split(g + (j + 2) // 4, (j + 2) % 4, a0, n0, src)
                    if not isinstance(g, int) or n0 + 4 * g + j + 2 < END_N:
                        split(g, n0 + j + 2)

                blocks(act, n, body, whole=1)

            act.preload_act_table_set("silu_and_others")
            norm(0, XN, NT, 0, ("x_in",))
            act.wait_ge(sem("params_out"), 5)
            f(cond[:, :, 0], PAR[:, 4, 64:72], ACT.Silu).then_inc(sem("cond"), 1)
            f(cond[:, :, 1], PAR[:, 4, 72:80], ACT.Silu).then_inc(sem("cond"), 1)
            act.wait_ge(sem("cond"), 2)
            f(CD4[:, :, 0:2], cond, ACT.Copy).then_inc(sem("small_high"), 1)
            f(SH[:, :, :], small_w, ACT.Copy).then_inc(sem("small_high"), 1)
            split(0, 0)
            split(0, 1)
            norm_high(0, NT)

            def conv(g, j):
                i = 4 * g + j
                split(g, CONV_N + j + 2)
                used(g, CONV_N + j)
                f(CT[:, j % 2, :], PS[:, j, :], ACT.Copy, scale=CW[:, ds(3 * CH + i, 1)])\
                    .then_inc(sem("tap"), 1)
                act.wait_ge(sem("conv_step"), 12 + 3 * i + 3)
                f(FT[:, i, :], CT[:, j % 2, :], ACT.Silu, bias=CW[:, ds(4 * CH + i, 1)])\
                    .then_inc(sem("conv_out"), 1)

            blocks(act, CH, conv)
            act.preload_act_table_set("exp_and_others")
            act.wait_ge(sem("conv_out"), CH)
            for i in range(16):
                if i > 3:
                    act.wait_ge(sem("qk_sum"), i - 3)
                f(arena(QE_ + (i % 4) * T, T), FT[:, i, :], ACT.Square).then_inc(sem("qk_square"), 1)
            act.wait_ge(sem("sp_abs"), 1)
            f(sp_e, sp_e, ACT.Exp, scale=-1.0).then_inc(sem("sp_exp"), 1)
            f(nega, head_log, ACT.Exp).then_inc(sem("sp_exp"), 1)
            f(beta, proj[:, :, 0:8], ACT.Exp, scale=-1.0).then_inc(sem("sp_exp"), 1)
            act.wait_ge(sem("cum_out"), 1)
            f(ecum, ncum, ACT.Exp, scale=-1.0).then_inc(sem("cum_exp"), 1)
            f(edec, edec, ACT.Exp).then_inc(sem("cum_exp"), 1)
            f(etot, PS[:, 5, 0:96].rearrange("p (a b) -> p a b", b=24), ACT.Exp).then_inc(sem("cum_exp"), 1)

            def four(q):
                return range(4 * q, 4 * q + 4)

            def tiles(at, q):
                return arena(at + q * 512, 512)

            for c in range(NT):
                tc = slice(c * P, (c + 1) * P)
                for q in range(2):
                    act.wait_ge(sem("d_arg"), 2 * c + q + 1)
                    for h in four(q):
                        m = f(arena(PP_ + h * P, P), arena(PP_ + h * P, P), ACT.Exp,
                              bias=ncum[:, c, h:h + 1])
                    m.then_inc(sem("d_exp"), 1)
                for level in range(1, LEVELS):
                    u = 2 * (c * (LEVELS - 1) + level - 1) + 1
                    for q in range(2):
                        act.wait_ge(sem("d_nt"), u + q)
                        if level == 1:
                            act.wait_ge(sem("d_level"), 2 * c * LEVELS + 2)
                        else:
                            act.wait_ge(sem("d_tnt"), u - 2 + q)
                        f(tiles(PP_, q), PS[:, 2 + q, :], ACT.Copy).then_inc(sem("d_nt_out"), 1)
                for q in range(2):
                    act.wait_ge(sem("d_w"), 2 * c + q + 1)
                    f(tiles(NW_, q), PS[:, 4 + q, :], ACT.Copy, scale=-1.0).then_inc(sem("d_w_out"), 1)
                for q in range(2):
                    act.wait_ge(sem("d_new"), 2 * c + q + 1)
                    f(tiles(VN_, q), PS[:, 6 + q, :], ACT.Copy).then_inc(sem("d_new_out"), 1)
                for q in range(2):
                    act.wait_ge(sem("d_o"), 2 * c + q + 1)
                    f(tiles(PP_, q), tiles(R_, q), ACT.Square).then_inc(sem("d_o_square"), 1)
                for q in range(2):
                    act.wait_ge(sem("d_o_turned"), 2 * c + q + 1)
                    f(FT[:, Q0 + 4 * q:Q0 + 4 * q + 4, tc], PS[:, 6 + q, :].rearrange("p (h t) -> p h t", t=P),
                      ACT.Copy, scale=PAR[:, 1, 68:69]).then_inc(sem("d_o_out"), 1)
                act.wait_ge(sem("s_turned"), c + 1)
                f(arena(NW_, 2 * P), PS[:, 2, 0:2 * P], ACT.Copy).then_inc(sem("s_b_out"), 1)
                for g in range(2):
                    act.wait_ge(sem("s_arg"), 2 * c + g + 1)
                    for h in range(8):
                        m = f(arena(QE_ + h * P, P), arena(QE_ + h * P, P), ACT.Exp,
                              bias=ncum[:, c, 8 + 8 * g + h:9 + 8 * g + h])
                    m.then_inc(sem("s_exp"), 1)
                    act.wait_ge(sem("y_turned"), 2 * c + g + 1)
                    f(FT[:, X0 + 4 * g:X0 + 4 * g + 4, tc], PS[:, g, :].rearrange("p (h t) -> p h t", t=P),
                      ACT.Copy).then_inc(sem("y_turned_out"), 1)
            act.preload_act_table_set("silu_and_others")

            def gated(g, j):
                split(g, Z_N + j + 2)
                used(g, Z_N + j)
                act.wait_ge(sem("z_step"), 4 * g + j + 1)
                f(arena(R_ + j * T, T), PS[:, j, :], ACT.Silu).then_inc(sem("z_silu"), 1)

            def gated_s(g, j):
                gated(g, j)
                i = 4 * g + j
                act.wait_ge(sem("z_step"), i + 5)
                f(arena(NM_ + i * T, T), FT[:, X0 + i, :], ACT.Square).then_inc(sem("y_square"), 1)

            for g in range(2):
                for j in range(4):
                    gated_s(g, j)
            for g in range(2, 4):
                for j in range(4):
                    gated(g, j)
            act.preload_act_table_set("natural_log_exp_and_others")
            for g in range(2):
                act.wait_ge(sem("y_sum"), 4 * g + 4)
                f(arena(QE_ + g * T, T), PS[:, 4 + g, :], ACT.Ln, scale=1.0 / 512, bias=eps_col)\
                    .then_inc(sem("y_ln"), 1)
                act.wait_ge(sem("y_ln"), 2 * g + 1)
                f(arena(QE_ + g * T, T), arena(QE_ + g * T, T), ACT.Exp, scale=-0.5)\
                    .then_inc(sem("y_ln"), 1)
            act.wait_ge(sem("z_step"), 20)
            for t in range(NT):
                act.dma_start(X1[:, t, :], x_rows[t]).then_inc(sem("x_again"), 16)
            act.dma_start(WB, a["post_mix_norm"].to_broadcast([P, D])).then_inc(sem("x_again"), 16)
            down(WO_N, WO_A, 16, arena(16 * T, 16, T), ("y_norm", lambda k: 8))

            def squares(n0, count, tiles_):
                used(0, n0 + count - 1)
                for t in range(NT):
                    f(XN[:, t, :], PS[:, 2 * t:2 * t + 2, :].rearrange("p a b -> p (a b)"), ACT.Square,
                      accum_out=sumsq2[:, tiles_ + t:tiles_ + t + 1]).then_inc(sem("p_square"), 1)

            squares(WO_N, 16, 0)
            norm(1, X1, NT, 4, ("x_res", 1))
            norm_high(1, NT)
            act.preload_act_table_set("silu_and_others")

            def up_split(q, j):
                act.wait_ge(sem(f"w_in{j % 4}"), 16 * q + 16 * ((UP_N + j) // 4 + 1))
                act.wait_ge(sem("w_used"), 4 * q + UP_N + j + (0 if j % 4 > 1 else -1))
                f(parts(j)[0], RAW[:, j % 4, :], ACT.Copy).then_inc(sem("w_high"), 1)

            def ffn(q, i, j, cg):
                up_split(q, j + 3)
                if j < 2:
                    used(q, UP_N + j)
                if j == 0:
                    f(CT[:, 0, :], PS[:, 0, :], ACT.Copy, scale=PAR[:, 3, ds(q, 1)])\
                        .then_inc(sem("ffn_tap"), 1)
                    act.wait_ge(sem("ffn_step"), 5 * q + 5 + 2)
                    f(GT_T, CT[:, 0, :], ACT.Silu, bias=PAR[:, 3, ds(q + 44, 1)]).then_inc(sem("ffn_gate"), 1)
                elif j == 1:
                    f(CT[:, 1, :], PS[:, 1, :], ACT.Identity, scale=PAR[:, 3, ds(q + 22, 1)],
                      bias=PAR[:, 3, ds(q + 66, 1)]).then_inc(sem("ffn_tap"), 1)
                elif i == 3 and j == 3:
                    mod_rows(q, j, cg)

            def mod_rows(q, j, cg):
                used(q, UP_N + j)
                f(MR[:, ds(cg * D, D)], PS[0:4, 4:6, :].rearrange("p a b -> p (a b)"), ACT.Copy)\
                    .then_inc(sem("mod_rows"), 1)

            up_split(0, 2)
            up_groups(act, ffn)
            up_split(0, 4 * FF + 3)
            split(0, DN_N)
            split(0, DN_N + 1)
            mod_rows(FF, 3, 5)
            act.wait_ge(sem("mod_out"), 1)
            act.wait_ge(sem("x_res"), 4)
            with nc.allow_non_contiguous_dma(reason="16 KB of modulation, once"):
                for v, first in enumerate((16, 40)):
                    act.dma_start(gmod[v].rearrange("(t p) -> p t", p=P), modT[:, first:first + 8, 0])\
                        .then_inc(sem("gmod_out"), 16)
            act.dma_start(WB, a["post_ffn_norm"].to_broadcast([P, D])).then_inc(sem("wb_in"), 16)
            down(DN_N, DN_A, FF, FFT, ("ffn_step", lambda k: 5 * k + 5 + 5))
            squares(DN_N, FF, 4)
            norm(2, X1, NT, 8, ("x_res", 5))
            for t in range(2):
                act.dma_start(arena(QT_, 2, D)[:, t, :], ctx_rows[t]).then_inc(sem(f"c_in{t}"), 16)
            act.wait_ge(sem("pad_out"), 16)
            act.dma_start(A[:, C2_:C2_ + 576], cst[:, COLMASK:FLIP]).then_inc(sem("c2_in"), 16)
            act.dma_start(FLP, cst[:, FLIP:NCST]).then_inc(sem("c2_in"), 16)
            norm(3, arena(QT_, 2, D), 2, 12, ("c_in",))
            norm_high(2, NT)
            act.wait_ge(sem("n_turned"), 24)
            for v in range(2):
                act.dma_start(arena(R1_ + 4096, 2, NT, T)[:, v], dft[v].rearrange("(k p) t -> p k t", p=P))\
                    .then_inc(sem("dft_in"), 16)
            norm_high(3, 2)
            for j in range(4):
                split(0, PR_N + j + 2)
                used(0, PR_N + j)
                f(arena(F_ + j * T, T), PS[:, j, :], ACT.Copy).then_inc(sem("pr_out"), 1)
            for part in range(3):
                for b in range(4):
                    split(0, PR_N + 4 + 4 * part + b + 2)
                used(0, PR_N + 4 + 4 * part + 3)
                for i in range(4 if part == 0 else 6):
                    at = [QK_, QK_ + 4 * T, V_][part] + i * T
                    f(arena(at, T), PS[:, BANKS[part][i][0], :], ACT.Copy).then_inc(sem("pr_out"), 1)
            for i in range(8):
                t, u = divmod(i, 2)
                act.wait_ge(sem("f_mix"), i + 1)
                f(arena(R1_ + t * 1024 + u * 512, 512), PS[:, 2 * (t % 2) + u, :], ACT.Copy)\
                    .then_inc(sem("f_mix_out"), 1)
            for gr in range(4):
                act.wait_ge(sem("f_done"), gr + 1)
                f(arena(F_ + gr * T, T), PS[:, 4 + gr, :], ACT.Copy).then_inc(sem("f_out"), 1)
            QT = arena(QT_, 4, T)
            KT = arena(KT_, 4, NKEY)
            for i in range(10):
                act.wait_ge(sem("qk_turned"), i + 1)
                src = PS[:, i % 4, :].rearrange("p (h t) -> p h t", t=P)
                dst = QT[:, :, i * P:(i + 1) * P] if i < 4 else KT[:, :, (i - 4) * P:(i - 3) * P]
                f(dst, src, ACT.Copy).then_inc(sem("qk_turned_out"), 1)
            act.preload_act_table_set("exp_and_others")

            def side_out(i):
                h, t = divmod(i, NT)
                act.wait_ge(sem("at_p_turned"), i + 1)
                if h > 1:
                    act.wait_ge(sem("at_o"), h - 1)
                f(probs_t(h)[:, 4:6, t * P:(t + 1) * P], turned(i)[1].rearrange("p (a b) -> p a b", b=P),
                  ACT.Copy).then_inc(sem("at_ctx_out"), 1)

            def head_out(h):
                act.wait_ge(sem("at_o"), h + 1)
                r = slice(DH * (h % 2), DH * (h % 2) + DH)
                f(QT[r, h // 2, :], PS[r, 7, :], ACT.Copy).then_inc(sem("at_o_out"), 1)

            for i in range(AH_ * NT):
                act.wait_ge(sem("at_max"), i + 1)
                if i > 1:
                    act.wait_ge(sem("at_p_turned"), i - 1)
                b = 2 * (i % 2)
                f(probs(i), PSF[:, b * 512:b * 512 + NKEY], ACT.Exp, bias=smax[:, i:i + 1],
                  accum_out=ssum[:, i:i + 1]).then_inc(sem("at_exp"), 1)
                if i:
                    side_out(i - 1)
                if i > NT and i % NT == 1:
                    head_out(i // NT - 1)
            side_out(AH_ * NT - 1)
            head_out(AH_ - 1)
            act.wait_ge(sem("at_o_out"), AH_)
            act.preload_act_table_set("sigmoid_and_others")

            def gate(g, j):
                split(g, GT_N + j + 2)
                used(g, GT_N + j)
                f(arena(R1_, 16, T)[:, 4 * g + j, :], PS[:, j, :], ACT.Sigmoid).then_inc(sem("gate_out"), 1)

            for k in range(4):
                f(AH[:, k, :], arena(F_ + k * T, T), ACT.Copy).then_inc(sem("branch_high"), 1)
            blocks(act, 16, gate)
            for k in range(4):
                f(HH[:, k, :], QT[:, k, :], ACT.Copy).then_inc(sem("branch_high"), 1)
            for n in range(8):
                split(0, FA_N + n + 2)
            used(0, W2_N - 1)
            act.wait_ge(sem("gmod_out"), 32)
            act.dma_start(WB, gmod[0:1, :].to_broadcast([P, D])).then_inc(sem("wb_in"), 16)
            down(W2_N, W2_A, 8, arena(MT_, 8, T), ("merge_out", lambda k: k + 1 if isinstance(k, int) else 8))
            act.preload_act_table_set("exp_and_others")
            norm(4, X1, NT, 14, ("x_res", 9))
            act.dma_start(WB, gmod[1:2, :].to_broadcast([P, D])).then_inc(sem("wb_in"), 16)
            norm_high(4, NT)

            def mlp(g, j):
                split(g, M1_N + j + 2)
                used(g, M1_N + j)
                act.wait_ge(sem("mlp_out"), 4 * g + j + 3)
                f(CT[:, j % 2, :], PS[:, j, :], ACT.Relu).then_inc(sem("mlp_relu"), 1)

            blocks(act, MF, mlp)
            down(M2_N, M2_A, MF, arena(M1_, MF, T), ("mlp_out", lambda k: MF + 4))

        @block.vector
        def _(dve):
            tt, ts, stt = dve.tensor_tensor, dve.tensor_scalar, dve.scalar_tensor_tensor
            own = [0]

            def step(ins):
                own[0] += 1
                ins.then_inc(sem("dve_own"), 1)
                dve.wait_ge(sem("dve_own"), own[0])

            dve.memset(half, -0.5).then_inc(sem("half"), 1)
            dve.memset(eps_col, EPS)
            dve.sem_inc(sem("w_low"), 4)
            dve.sem_inc(sem("w_used"), 2)
            dve.sem_inc(sem("conv_step"), 12)
            dve.sem_inc(sem("z_step"), 4)
            dve.sem_inc(sem("ffn_step"), 5)
            dve.sem_inc(sem("mod_rows"), 1)
            dve.sem_inc(sem("mlp_out"), 4)
            dve.sem_inc(sem("gate_out"), 4)

            def split(g, off):
                dve.wait_ge(sem("w_high"), 4 * g + off + 1)
                tt(WL[:, off % 2, :], RAW[:, off % 4, :], WH[:, off % 2, :].bitcast(F32),
                   ALU.subtract).then_inc(sem("w_low"), 1)

            def used(g, off):
                dve.wait_ge(sem("w_used"), 4 * g + off + 1 + 2)

            def act_split(g, j, a0, src):
                dve.wait_ge(sem("a_high"), 4 * g + j + a0 + 1)
                r = (a0 + j) % 4
                tt(AL[:, r, :], src[:, 4 * g + j, :], AH[:, r, :].bitcast(F32), ALU.subtract)\
                    .then_inc(sem("a_low"), 1)

            def scaled(job, x, xn, nt, tiles):
                for t in range(nt):
                    dve.wait_ge(sem("n_rstd"), tiles + t + 1)
                    ts(xn[:, t, :], x[:, t, :], rstd[:, tiles + t:tiles + t + 1], None, ALU.mult)\
                        .then_inc(sem("n_x"), 1)

            def norm_low(job, nt, gain, shift=None):
                hh, hl = HH, HL
                if job == 3:
                    hh, hl = (v[:, :, :].rearrange("p a b -> p (a b)").rearrange("p (k t) -> p k t", t=CTX)
                              for v in (AH, AL))

                def low(k):
                    dve.wait_ge(sem("n_high"), 8 * job + k + 1)
                    tt(hl[:, k, :], HT[:, k % 2, 0:nt * P], hh[:, k, :].bitcast(F32), ALU.subtract)\
                        .then_inc(sem("n_low"), 1)

                for k in range(KD):
                    dve.wait_ge(sem("n_turned"), 8 * job + k + 1)
                    src = PS[:, 4 + k % 4, 0:nt * P]
                    if 8 * job + k > 1:
                        dve.wait_ge(sem("n_low"), 8 * job + k - 1)
                    if shift is None:
                        m = ts(HT[:, k % 2, 0:nt * P], src, gain(k), None, ALU.mult)
                    else:
                        m = ts(HT[:, k % 2, 0:nt * P], src, gain(k), shift(k), ALU.mult, ALU.add)
                    m.then_inc(sem("n_value"), 1)
                    if k:
                        low(k - 1)
                low(KD - 1)

            def down(n0, a0, n, src):
                for j in range(2):
                    act_split(0, j, a0, src)

                def body(g, j):
                    if not isinstance(g, int) or 4 * g + j + 2 < n:
                        act_split(g + (j + 2) // 4, (j + 2) % 4, a0, src)
                    if not isinstance(g, int) or n0 + 4 * g + j + 2 < END_N:
                        split(g, n0 + j + 2)

                blocks(dve, n, body, whole=1)

            def residual(f0, n0, count, wb, normed):
                used(0, n0 + count - 1)
                dve.wait_ge(sem(wb[0]), wb[1])
                for t in range(NT):
                    o = PS[:, 2 * t:2 * t + 2, :].rearrange("p a b -> p (a b)")
                    if t:
                        dve.wait_ge(sem("x_res"), NT * f0 + t)
                    if normed is not None:
                        dve.wait_ge(sem("p_rstd"), normed + t + 1)
                        step(stt(YT, o, rstd2[:, normed + t:normed + t + 1], WB, ALU.mult, ALU.mult))
                    else:
                        step(tt(YT, o, WB, ALU.mult))
                    tt(X1[:, t, :], X1[:, t, :], YT, ALU.add).then_inc(sem("x_res"), 1)

            dve.wait_ge(sem("params_turned"), 1)
            for s, r in enumerate(STAGED):
                dve.tensor_copy(PAR[:, s, 0:r], PS[:, s // 4, (s % 4) * P:(s % 4) * P + r])\
                    .then_inc(sem("params_out"), 1)
            dve.wait_ge(sem("params_out"), 5)
            for k in range(4):
                dve.tensor_copy(CW[:, k * CH:k * CH + 24], PAR[:, 0, k * 24:(k + 1) * 24])
                dve.tensor_copy(CW[:, k * CH + 24:(k + 1) * CH], PAR[:, 1, k * 12:(k + 1) * 12])
            dve.memset(CW[:, 4 * CH:4 * CH + 24], 0.0)
            step(dve.tensor_copy(CW[:, 4 * CH + 24:5 * CH], PAR[:, 1, 48:60]))
            scaled(0, XN, XN, NT, 0)
            split(0, 0)
            dve.wait_ge(sem("small_high"), 2)
            tt(CD4[:, :, 2:4], cond, CD4[:, :, 0:2].bitcast(F32), ALU.subtract)
            tt(join, IDN[0:4, 0:2], IDN[0:4, 2:4], ALU.add).then_inc(sem("join_ready"), 1)
            tt(SL[:, :, :], small_w, SH[:, :, :].bitcast(F32), ALU.subtract).then_inc(sem("small_low"), 1)
            split(0, 1)
            norm_low(0, NT, lambda k: PAR[:, 1, 60 + k:61 + k])

            def conv(g, j):
                i = 4 * g + j
                split(g, CONV_N + j + 2)
                for k in range(3):
                    lag = k + 1
                    if k == 0:
                        dve.wait_ge(sem("tap"), i + 1)
                    else:
                        dve.wait_ge(sem("conv_step"), 12 + 3 * i + k)
                    o = CT[:, j % 2, lag:T]
                    stt(o, PS[:, j, 0:T - lag], CW[:, ds((3 - lag) * CH + i, 1)], o, ALU.mult, ALU.add)\
                        .then_inc(sem("conv_step"), 1)

            blocks(dve, CH, conv)
            dve.wait_ge(sem("proj_done"), 1)
            step(dve.tensor_copy(proj, PS[:, 7, 0:P].rearrange("p (a b) -> p a b", b=32)))
            step(tt(sp_x, proj[:, :, 8:32], each(head_bias, NT), ALU.add))
            step(ts(sp_q, sp_x, -1.0, None, ALU.mult))
            tt(sp_e, sp_x, sp_q, ALU.max).then_inc(sem("sp_abs"), 1)
            dve.wait_ge(sem("sp_exp"), 3)
            step(ts(sp_s, sp_e, 2.0, None, ALU.add))
            step(dve.reciprocal(sp_s, sp_s))
            step(tt(sp_s, sp_s, sp_e, ALU.mult))
            step(tt(sp_q, sp_s, sp_s, ALU.mult))
            step(ts(soft, sp_q, 1.0 / 17, 1.0 / 15, ALU.mult, ALU.add))
            for n in (13, 11, 9, 7, 5, 3, 1):
                step(tt(soft, soft, sp_q, ALU.mult))
                step(ts(soft, soft, 1.0 / n, None, ALU.add))
            step(tt(soft, soft, sp_s, ALU.mult))
            step(ts(sp_x, sp_x, 0.0, None, ALU.max))
            step(stt(soft, soft, 2.0, sp_x, ALU.mult, ALU.add))
            step(ts(nega, nega, -1.0, None, ALU.mult))
            step(tt(logdec, soft, each(nega, NT), ALU.mult))
            step(ts(beta, beta, 1.0, None, ALU.add))
            dve.reciprocal(beta, beta).then_inc(sem("logdec_ready"), 1)
            dve.wait_ge(sem("logdec_ready"), 1)
            dve.wait_ge(sem("cum_done"), 1)
            cum = PS[:, 4, 0:96].rearrange("p (a b) -> p a b", b=24)
            step(ts(ncum, cum, -1.0, None, ALU.mult))
            tt(edec, PS[:, 5, 0:96].rearrange("p (a b) -> p a b", b=24), ncum, ALU.add)\
                .then_inc(sem("cum_out"), 1)
            dve.wait_ge(sem("qk_sum"), 16)
            ts(qks, PS[:, 6, 0:2 * 64].rearrange("p (a b) -> p a b", b=2)[:, :, 0]
               .rearrange("p (a b) -> p a b", b=16), EPS, None, ALU.add).then_inc(sem("qk_eps"), 1)
            dve.wait_ge(sem("qk_pow"), 1)
            dve.wait_ge(sem("cum_exp"), 3)
            rk = qkr[:, :, 8:16]
            ts(nrk, rk, -1.0, None, ALU.mult)
            step(tt(brk, rk, beta, ALU.mult))
            tt(kbs, brk, ecum[:, :, 0:8], ALU.mult)
            tt(kds, rk, edec[:, :, 0:8], ALU.mult)
            step(ts(qkr[:, :, 0:8], qkr[:, :, 0:8], float(P) ** -0.5, None, ALU.mult))
            step(tt(rq2, qkr[:, :, 0:8], qkr[:, :, 0:8], ALU.mult))
            ts(rq2, rq2, 1.0 / P, None, ALU.mult).then_inc(sem("scales_ready"), 1)
            dve.wait_ge(sem("scales_ready"), 1)
            dve.wait_ge(sem("levels_in"), 1)

            def four(q):
                return range(4 * q, 4 * q + 4)

            def tiles(at, q):
                return arena(at + q * 512, 4, P)

            def bank(b):
                return PS[:, b, :].rearrange("p (h t) -> p h t", t=P)

            def heads(v, c, q):
                return up_to(v[:, c, 4 * q:4 * q + 4], 4)

            for c in range(NT):
                tc = slice(c * P, (c + 1) * P)
                for q in range(2):
                    dve.wait_ge(sem("d_cum"), 2 * c + q + 1)
                    tt(tiles(PP_, q), bank(q), each(NGM, 4), ALU.add).then_inc(sem("d_arg"), 1)
                for q in range(2):
                    dve.wait_ge(sem("d_exp"), 2 * c + q + 1)
                    dve.wait_ge(sem("d_gram"), 2 * c + q + 1)
                    step(tt(tiles(NM_, q), tiles(PP_, q), bank(2 + q), ALU.mult))
                    for h in four(q):
                        hc = slice((h % 4) * P, (h % 4 + 1) * P)
                        stt(arena(NM_ + h * P, P), PS[:, 4 + q, hc], nrk[:, c, h:h + 1],
                            arena(NM_ + h * P, P), ALU.mult, ALU.mult)
                        m = stt(arena(QE_ + h * P, P), PS[:, 6 + q, hc], rk[:, c, h:h + 1],
                                arena(PP_ + h * P, P), ALU.mult, ALU.mult)
                    step(m)
                    step(dve.tensor_copy(tiles(R_, q), each(IDN, 4)))
                    dve.copy_predicated(tiles(R_, q), each(LV[:, 1, :], 4), tiles(NM_, q))\
                        .then_inc(sem("d_r0"), 1)
                for q in range(2):
                    dve.wait_ge(sem("d_r0_turned"), 2 * c + q + 1)
                    dve.tensor_copy(tiles(TT_, q), bank(q)).then_inc(sem("d_level"), 1)
                for level in range(1, LEVELS):
                    u = 2 * (c * (LEVELS - 1) + level - 1) + 1
                    for q in range(2):
                        dve.wait_ge(sem("d_tnt"), u + q)
                        if level < LEVELS - 1:
                            dve.copy_predicated(tiles(TT_, q), each(LV[:, 2 * level, :], 4), bank(4 + q))
                        dve.copy_predicated(tiles(R_, q), each(LV[:, 2 * level + 1, :], 4), bank(6 + q))\
                            .then_inc(sem("d_level"), 1)
                for q in range(2):
                    dve.wait_ge(sem("d_kv_turned"), 2 * c + q + 1)
                    tt(tiles(TT_, q), bank(q), heads(kbs, c, q), ALU.mult)
                    tt(tiles(NM_, q), bank(q), heads(kds, c, q), ALU.mult)
                    tt(tiles(PP_, q), bank(2 + q), heads(beta, c, q), ALU.mult).then_inc(sem("d_kv_out"), 1)
                for q in range(2):
                    dve.wait_ge(sem("d_out"), 2 * c + q + 1)
                    if c:
                        step(tt(tiles(R_, q), bank(q), heads(ecum, c, q), ALU.mult))
                        tt(tiles(R_, q), tiles(R_, q), bank(2 + q), ALU.add).then_inc(sem("d_o"), 1)
                        for h in four(q):
                            m = stt(arena(SD_ + h * P, P), arena(SD_ + h * P, P), etot[:, c, h:h + 1],
                                    PS[:, 4 + q, (h % 4) * P:(h % 4 + 1) * P], ALU.mult, ALU.add)
                    else:
                        dve.tensor_copy(tiles(R_, q), bank(2 + q)).then_inc(sem("d_o"), 1)
                        m = dve.tensor_copy(tiles(SD_, q), bank(4 + q))
                    m.then_inc(sem("d_state"), 1)
                for q in range(2):
                    hs = slice(4 * q, 4 * q + 4)
                    dve.wait_ge(sem("d_o_square"), 2 * c + q + 1)
                    step(dve.tensor_reduce(oss[:, c, hs], tiles(PP_, q), AX.X, ALU.add))
                    step(tt(oss[:, c, hs], oss[:, c, hs], rq2[:, c, hs], ALU.mult))
                    ts(oss[:, c, hs], oss[:, c, hs], EPS, None, ALU.add).then_inc(sem("o_eps"), 1)
                for q in range(2):
                    hs = slice(4 * q, 4 * q + 4)
                    dve.wait_ge(sem("o_pow"), 2 * c + q + 1)
                    step(tt(ors[:, c, hs], ors[:, c, hs], qkr[:, c, hs], ALU.mult))
                    tt(tiles(R_, q), tiles(R_, q), heads(ors, c, q), ALU.mult).then_inc(sem("d_normed"), 1)
                dve.wait_ge(sem("s_turned"), c + 1)
                dve.wait_ge(sem("d_o_turned"), 2 * c + 2)

                def wide(v, lo):
                    return v[:, c, lo:lo + HS].unsqueeze(2).to_broadcast([P, HS, PD])

                xt = PS[:, 0:2, :].rearrange("p a b -> p (a b)").rearrange("p (h d) -> p h d", d=PD)
                step(tt(arena(TT_, HS, PD), xt, wide(soft, 8), ALU.mult))
                tt(arena(NM_, HS, PD), arena(TT_, HS, PD), wide(edec, 8), ALU.mult)
                tt(arena(PP_, HS, PD), xt, skip_d.unsqueeze(2).to_broadcast([P, HS, PD]), ALU.mult)
                dve.wait_ge(sem("s_b_out"), c + 1)
                for g in range(2):
                    dve.wait_ge(sem("s_cum"), 2 * c + g + 1)
                    for r in range(2):
                        m = tt(tiles(QE_, r), bank(4 + r), each(NGM, 4), ALU.add)
                    m.then_inc(sem("s_arg"), 1)
                    dve.wait_ge(sem("s_exp"), 2 * c + g + 1)
                    if g:
                        dve.wait_ge(sem("s_sum"), 2 * c + g)
                    for r in range(2):
                        m = tt(tiles(R_, r), tiles(QE_, r), each(PS[:, 3, g * P:(g + 1) * P], 4), ALU.mult)
                    m.then_inc(sem("s_m"), 1)
                    dve.wait_ge(sem("s_sum"), 2 * c + g + 1)
                    y, xd = arena(VN_ + g * 512, 8, PD), arena(PP_ + g * 512, 8, PD)
                    st = arena(SS_ + g * 512, 8, PD)

                    def rate(v):
                        return v[:, c, 8 + 8 * g:16 + 8 * g].unsqueeze(2).to_broadcast([P, 8, PD])

                    def whole(b):
                        return PS[:, b, :].rearrange("p (h d) -> p h d", d=PD)

                    step(tt(y, whole(6), xd, ALU.add))
                    if c:
                        step(tt(xd, whole(7), rate(ecum), ALU.mult))
                        tt(y, y, xd, ALU.add)
                        step(tt(st, st, rate(etot), ALU.mult))
                        m = tt(st, st, whole(2), ALU.add)
                    else:
                        m = dve.tensor_copy(st, whole(2))
                    m.then_inc(sem("s_y"), 1)

            def gated(g, j):
                split(g, Z_N + j + 2)
                dve.wait_ge(sem("z_silu"), 4 * g + j + 1)
                i = 4 * g + j
                src, dst = (X0 + i, X0 + i) if i < 8 else (i - 8, i + 8)
                tt(FT[:, dst, :], FT[:, src, :], arena(R_ + j * T, T), ALU.mult).then_inc(sem("z_step"), 1)

            for g in range(4):
                for j in range(4):
                    gated(g, j)
            for i in range(8):
                if i % 4 == 0:
                    dve.wait_ge(sem("y_ln"), 2 * (i // 4) + 2)
                stt(FT[:, X0 + i, :], FT[:, X0 + i, :], PAR[:, 1, 69 + i:70 + i], arena(QE_ + (i // 4) * T, T),
                    ALU.mult, ALU.mult).then_inc(sem("y_norm"), 1)
            down(WO_N, WO_A, 16, arena(16 * T, 16, T))
            residual(0, WO_N, 16, ("x_again", 80), 0)
            scaled(1, X1, XN, NT, 4)
            norm_low(1, NT, lambda k: PAR[:, 2, 88 + k:89 + k])

            def up_split(q, j):
                dve.wait_ge(sem("w_high"), 4 * q + UP_N + j + 1)
                wh, wl = parts(j)
                tt(wl, RAW[:, j % 4, :], wh.bitcast(F32), ALU.subtract).then_inc(sem("w_low"), 1)

            def ffn(q, i, j, cg):
                up_split(q, j + 3)
                base = 5 * q + 5
                if j < 2:
                    dve.wait_ge(sem("ffn_tap"), 2 * q + j + 1)
                    for lag in (1, 2):
                        if lag == 2:
                            dve.wait_ge(sem("ffn_step"), base + 2 * j + 1)
                        o = CT[:, j, lag:T]
                        w = PAR[:, 2, ds(q + (2 - lag) * 2 * FF + j * FF, 1)]
                        stt(o, PS[:, j, 0:T - lag], w, o, ALU.mult, ALU.add).then_inc(sem("ffn_step"), 1)
                if j == 1:
                    dve.wait_ge(sem("ffn_gate"), q + 1)
                    dve.wait_ge(sem("ffn_step"), base + 4)
                    tt(FFT[:, q, :], CT[:, 1, :], GT_T, ALU.mult).then_inc(sem("ffn_step"), 1)

            up_split(0, 2)
            up_groups(dve, ffn)
            up_split(0, 4 * FF + 3)
            split(0, DN_N)
            split(0, DN_N + 1)
            dve.wait_ge(sem("mod_turned"), 1)
            tt(modT, PS[:, 6, 0:2 * NADA].rearrange("p (a b) -> p a b", b=2),
               PAR[:, 4, 0:NADA].unsqueeze(2).to_broadcast([P, NADA, 2]), ALU.add).then_inc(sem("mod_out"), 1)
            dve.wait_ge(sem("mod_out"), 1)
            for r, (gain, scale, who) in enumerate(((48, 8, 0), (48, 8, 1), (56, 32, 0))):
                stt_in = modT[:, scale:scale + 8, who]
                step(stt(affine[:, r, :], stt_in, 1.0, PAR[:, 4, gain:gain + 8], ALU.add, ALU.mult))
            down(DN_N, DN_A, FF, FFT)
            residual(1, DN_N, FF, ("wb_in", 16), 4)
            XC = arena(QT_, 2, D)
            scaled(2, X1, XN, NT, 8)
            scaled(3, XC, XC, 2, 12)
            norm_low(2, NT, lambda k: affine[:, 0, k:k + 1], lambda k: modT[:, k, 0:1])
            norm_low(3, 2, lambda k: affine[:, 1, k:k + 1], lambda k: modT[:, k, 1:2])
            for n in range(16):
                split(0, PR_N + n + 2)
            QK = arena(QK_, 10, AH_, DH)
            COS = arena(C2_ + 320, NT, 2, 16)
            SIN = arena(C2_ + 448, NT, 2, 16)
            sq = arena(QS_, AH_, DH)
            dve.wait_ge(sem("pr_out"), 14)
            dve.wait_ge(sem("c2_in"), 32)
            dve.wait_ge(sem("qkg_in"), 32)
            for i in range(10):
                step(tt(sq, QK[:, i], QK[:, i], ALU.mult))
                step(dve.tensor_reduce(qkss[:, i, :], sq, AX.X, ALU.add))
                ts(qkss[:, i, :], qkss[:, i, :], 1.0 / DH, EPS, ALU.mult, ALU.add).then_inc(sem("qk_ms"), 1)
            for i in range(10):
                gain = qkg[:, 0:DH] if i < 4 else qkg[:, DH:2 * DH]
                dve.wait_ge(sem("qk_rstd"), i + 1)
                step(tt(QK[:, i], QK[:, i], qkrs[:, i, :].unsqueeze(2).to_broadcast([P, AH_, DH]), ALU.mult))
                m = tt(QK[:, i], QK[:, i], gain.unsqueeze(1).to_broadcast([P, AH_, DH]), ALU.mult)
                if i < 8:
                    step(m)
                    v = QK[:, i].rearrange("p h (a s d) -> p h a s d", a=2, s=2)
                    x0, x1 = v[:, :, :, 0, :], v[:, :, :, 1, :]
                    cs, sn = (w[:, i % 4].unsqueeze(1).to_broadcast([P, AH_, 2, 16]) for w in (COS, SIN))
                    a0 = arena(QS_, AH_, 32).rearrange("p h (a d) -> p h a d", a=2)
                    a1 = arena(QS_ + 256, AH_, 32).rearrange("p h (a d) -> p h a d", a=2)
                    tt(a0, x0, sn, ALU.mult)
                    step(tt(a1, x1, sn, ALU.mult))
                    step(tt(x0, x0, cs, ALU.mult))
                    step(tt(x1, x1, cs, ALU.mult))
                    tt(x0, x0, a1, ALU.subtract)
                    m = tt(x1, x1, a0, ALU.add)
                m.then_inc(sem("qk_ready"), 1)
            for i in range(AH_ * NT + 2):
                if 0 < i < AH_ * NT + 1:
                    k = i - 1
                    dve.wait_ge(sem("at_exp"), k + 1)
                    step(dve.reciprocal(srec[:, k:k + 1], ssum[:, k:k + 1]))
                    ts(probs(k), probs(k), srec[:, k:k + 1], None, ALU.mult).then_inc(sem("at_scaled"), 1)
                if i < AH_ * NT:
                    b = 2 * (i % 2)
                    dve.wait_ge(sem("at_scores"), i + 1)
                    dve.tensor_reduce(smax[:, i:i + 1], PSF[:, b * 512:b * 512 + NKEY], AX.X, ALU.max,
                                      negate=True).then_inc(sem("at_max"), 1)
                if i > 1:
                    k = i - 2
                    h, t = divmod(k, NT)
                    dve.wait_ge(sem("at_p_turned"), k + 1)
                    if h > 1:
                        dve.wait_ge(sem("at_o"), h - 1)
                    dve.tensor_copy(probs_t(h)[:, 0:4, t * P:(t + 1) * P],
                                    turned(k)[0].rearrange("p (a b) -> p a b", b=P))\
                        .then_inc(sem("at_main_out"), 1)
            for k in range(4):
                dve.wait_ge(sem("branch_high"), k + 1)
                tt(AL[:, k, :], arena(F_ + k * T, T), AH[:, k, :].bitcast(F32), ALU.subtract)\
                    .then_inc(sem("branch_low"), 1)

            def gate(g, j):
                split(g, GT_N + j + 2)

            blocks(dve, 16, gate)
            for k in range(4):
                dve.wait_ge(sem("branch_high"), k + 5)
                tt(HL[:, k, :], arena(QT_, 4, T)[:, k, :], HH[:, k, :].bitcast(F32), ALU.subtract)\
                    .then_inc(sem("branch_low"), 1)
            G = arena(R1_, 16, T)
            MT = arena(MT_, 8, T)
            mg = arena(KT_, 2, T)
            for n in range(8):
                split(0, FA_N + n + 2)
                if n % 2:
                    used(0, FA_N + n)
                    for mm in range(2):
                        m = n - 1 + mm
                        if m:
                            dve.wait_ge(sem("merge_out"), m)
                        tt(mg[:, 0, :], PS[:, 2 * mm, :], G[:, m, :], ALU.mult)
                        step(tt(mg[:, 1, :], PS[:, 2 * mm + 1, :], G[:, 8 + m, :], ALU.mult))
                        tt(MT[:, m, :], mg[:, 0, :], mg[:, 1, :], ALU.add).then_inc(sem("merge_out"), 1)
            down(W2_N, W2_A, 8, MT)
            residual(2, W2_N, 8, ("wb_in", 32), None)
            scaled(4, X1, XN, NT, 14)
            norm_low(4, NT, lambda k: affine[:, 2, k:k + 1], lambda k: modT[:, 24 + k, 0:1])
            M1 = arena(M1_, MF, T)

            def mlp(g, j):
                split(g, M1_N + j + 2)
                dve.wait_ge(sem("mlp_relu"), 4 * g + j + 1)
                tt(M1[:, 4 * g + j, :], CT[:, j % 2, :], CT[:, j % 2, :], ALU.mult)\
                    .then_inc(sem("mlp_out"), 1)

            blocks(dve, MF, mlp)
            down(M2_N, M2_A, MF, M1)
            residual(3, M2_N, MF, ("wb_in", 48), None)

        @block.gpsimd
        def _(pool):
            own = [0]

            def step(ins):
                own[0] += 1
                ins.then_inc(sem("pool_own"), 1)
                pool.wait_ge(sem("pool_own"), own[0])

            def rstds(tiles, n):
                for t in range(tiles, tiles + n):
                    pool.wait_ge(sem("n_square"), t + 1)
                    step(pool.tensor_scalar(meansq[:, t:t + 1], sumsq[:, t:t + 1], 1.0 / D, EPS,
                                            ALU.mult, ALU.add))
                    pool.tensor_tensor(rstd[:, t:t + 1], meansq[:, t:t + 1], half[:, 0:1], ALU.pow)\
                        .then_inc(sem("n_rstd"), 1)

            def rstds2(tiles):
                for t in range(tiles, tiles + 4):
                    pool.wait_ge(sem("p_square"), t + 1)
                    step(pool.tensor_scalar(meansq2[:, t:t + 1], sumsq2[:, t:t + 1], 1.0 / D, EPS,
                                            ALU.mult, ALU.add))
                    pool.tensor_tensor(rstd2[:, t:t + 1], meansq2[:, t:t + 1], half[:, 0:1], ALU.pow)\
                        .then_inc(sem("p_rstd"), 1)

            pool.wait_ge(sem("half"), 1)
            rstds(0, 4)
            pad = A[0:120, C2_:C2_ + P]
            step(pool.memset(pad, 0.0))
            pool.dma_start(pad[:, 48:79], a["rpb_2"][0].rearrange("h r c -> (h r) c"))\
                .then_inc(sem("pad_in"), 16)
            pool.wait_ge(sem("pad_in"), 16)
            pool.dma_start(gpad.rearrange("h r c -> (h r) c"), pad).then_inc(sem("pad_out"), 16)
            pool.wait_ge(sem("consts_in"), CONSTS * 16)
            pool.tensor_copy(LV[:, :, :].rearrange("p a b -> p (a b)"), LVF).then_inc(sem("levels_in"), 1)
            pool.wait_ge(sem("qk_eps"), 1)
            pool.tensor_tensor(qkr, qks, half.rearrange("p (a b) -> p a b", b=16), ALU.pow)\
                .then_inc(sem("qk_pow"), 1)
            for i in range(2 * NT):
                c, q = divmod(i, 2)
                hs = slice(4 * q, 4 * q + 4)
                pool.wait_ge(sem("o_eps"), i + 1)
                pool.tensor_tensor(ors[:, c, hs], oss[:, c, hs], half[:, 0:4], ALU.pow)\
                    .then_inc(sem("o_pow"), 1)
            rstds2(0)
            rstds(4, 4)
            rstds2(4)
            rstds(8, 4)
            rstds(12, 2)
            for n, name in enumerate(("q_norm_g_2", "k_norm_g_2")):
                pool.dma_start(qkg[:, n * DH:(n + 1) * DH], a[name].to_broadcast([P, DH]))\
                    .then_inc(sem("qkg_raw"), 16)
            pool.wait_ge(sem("qkg_raw"), 32)
            pool.tensor_scalar(qkg[:, 0:DH], qkg[:, 0:DH], DH ** -0.5, 0.0, ALU.mult, ALU.add)\
                .then_inc(sem("qkg_in"), 32)
            for i in range(10):
                pool.wait_ge(sem("qk_ms"), i + 1)
                pool.tensor_tensor(qkrs[:, i, :], qkss[:, i, :], half[:, 0:AH_], ALU.pow)\
                    .then_inc(sem("qk_rstd"), 1)
            pool.wait_ge(sem("pad_out"), 16)
            pool.wait_ge(sem("f_done"), 4)
            for h in range(AH_):
                if h > 1:
                    pool.wait_ge(sem("at_scores"), NT * (h - 1))
                buf = arena(AG_ + (h % 2) * 1024, 16, GRID)
                for u in range(2):
                    src = bass.AP(gpad.tensor, h * 15 * P, [[1, GRID], [P, 15], [1, GRID]])
                    pool.dma_start(buf[u * GRID:(u + 1) * GRID, u:u + 15, :], src)\
                        .then_inc(sem(f"bias_in{h % 2}"), 16)
                pool.wait_ge(sem(f"bias_in{h % 2}"), 32 * (h // 2 + 1))
                pool.tensor_tensor(buf[:, 1:15, :], buf[:, 1:15, :],
                                   arena(C2_, GRID).unsqueeze(1).to_broadcast([P, 14, GRID]), ALU.add)\
                    .then_inc(sem("bias_ready"), 1)
            rstds(14, 4)


NAMES = ["x", "pre_mix_norm", "w_in", "gdn_conv_w", "gdn_a_log", "gdn_dt_bias", "gdn_norm_w",
         "ssd_conv_w", "ssd_conv_b", "ssd_a_log", "ssd_dt_bias", "ssd_d", "ssd_norm_w", "w_out",
         "post_mix_norm", "pre_ffn_norm", "w_up", "ffn_conv_w", "ffn_conv_b", "w_down",
         "post_ffn_norm", "c_2", "ctx_2", "c_ctx_2", "w_ada_2", "b_ada_2", "norm1_g_2", "norm2_g_2",
         "w_in_2", "q_norm_g_2", "k_norm_g_2", "rpb_2", "w_branch_gate_2", "w_fourier_out_2",
         "w_attn_out_2", "w_out_2", "w_mlp1_2", "w_mlp2_2"]


def kernel(**inputs):
    import concourse.bacc as bacc
    from concourse.bass_utils import run_bass_kernel_spmd

    nc = bacc.Bacc("TRN2", target_bir_lowering=False, num_devices=1)
    arrays, a = {}, {}
    for name in NAMES:
        arrays[name] = np.ascontiguousarray(inputs[name])
        a[name] = nc.dram_tensor(name, arrays[name].shape, F32, kind="ExternalInput").ap()
    for name, v in (("constants", constants()), ("transforms", transforms())):
        arrays[name] = v
        a[name] = nc.dram_tensor(name, v.shape, F32, kind="ExternalInput").ap()
    gmod = nc.dram_tensor("modulation_rows", (2, D), F32, kind="Internal").ap()
    gpad = nc.dram_tensor("padded_bias", (AH_, 15, P), F32, kind="Internal").ap()
    out = nc.dram_tensor("result", (1, T, D), F32, kind="ExternalOutput").ap()
    program(nc, a, a["constants"], a["transforms"], gmod, gpad, out)
    return run_bass_kernel_spmd(nc, [arrays], core_ids=[0]).results[0]["result"]
```

```python
from contextlib import ExitStack

import concourse.bass as bass
import numpy as np
from concourse import mybir

F32 = mybir.dt.float32
F32R = mybir.dt.float32r
ACT = mybir.ActivationFunctionType
ALU = mybir.AluOpType
AX = mybir.AxisListType
ds = bass.ds

P = 128
T = 512
NT = T // P
D = 1024
KD = D // P
H = 8
HS = 16
PD = 64
CH = 36
Q0, K0, V0, X0, B0, C0 = 0, 8, 16, 24, 32, 34
FF = 22
MF = 32
NADA = 48
EPS = 1e-6
LEVELS = 7
NEG = -1e30
GRID = 64
AH_ = 8
DH = 64
CTX = 256
NKEY = T + CTX

CONV_N = 0
Z_N = CONV_N + CH
WO_N = Z_N + 16
UP_N = WO_N + 16
DN_N = UP_N + 2 * FF + NADA
PR_N = DN_N + FF
GT_N = PR_N + 16
FA_N = GT_N + 16
W2_N = FA_N + 8
M1_N = W2_N + 8
M2_N = M1_N + MF
END_N = M2_N + MF
WO_A, DN_A, W2_A, M2_A = 0, 16, 16 + FF, 24 + FF


def constants():
    i = np.arange(P)
    ident = np.eye(P)
    upper = (i[:, None] <= i[None, :]).astype(np.float64)
    cols = [ident, upper, np.ones((P, P)), np.where(upper > 0, 0.0, NEG)]
    for level in range(LEVELS):
        s = 1 << level
        pair = (i[:, None] // (2 * s) == i[None, :] // (2 * s))
        low = pair & (i[:, None] % (2 * s) >= s) & (i[None, :] % (2 * s) < s)
        cols += [low.astype(np.float64), low.T.astype(np.float64)]
    cc = GRID - 1 - i % GRID
    start = np.clip(cc - 8, 0, GRID - 16)
    c = np.arange(GRID)
    cols.append(np.where((c[None] >= start[:, None]) & (c[None] < start[:, None] + 16), 0.0, NEG))
    ang = 2 * np.pi * np.outer(i, i) / P
    cols += [np.cos(ang), np.sin(ang)]
    inv = 10000.0 ** (-np.arange(0, 32, 2, dtype=np.float64) / 32)
    for fn in (np.cos, np.sin):
        for t in range(NT):
            tok = t * P + i
            a = np.stack([np.outer(tok // GRID, inv), np.outer(tok % GRID, inv)], 1)
            cols.append(fn(a).reshape(P, 32))
    flip = (i[:, None] // GRID == i[None, :] // GRID) & ((i[:, None] + i[None, :]) % GRID == GRID - 1)
    cols.append(flip.astype(np.float64))
    return np.concatenate(cols, 1).astype(np.float32)


def transforms():
    i = np.arange(T)
    ang = 2 * np.pi * (np.outer(i, i) % T) / T
    scale = (T * P) ** -0.5
    return np.stack([np.cos(ang) * scale, -np.sin(ang) * scale]).astype(np.float32)


LEVEL = 4 * P
COLMASK = LEVEL + 2 * LEVELS * P
DFT = COLMASK + GRID
COS = DFT + 2 * P
SIN = COS + NT * 32
FLIP = SIN + NT * 32
NCST = FLIP + P

ARENA = 28800
FT_ = 0
M_ = CH * T
QE_, R_, TT_, NM_, PP_, NW_, VN_, SD_, SS_ = (M_ + 1024 * i for i in range(9))
XN_ = M_
STG_ = M_ + 4096
LVL_ = STG_ + 640
CT_ = LVL_ + 2 * LEVELS * P
HT_ = CT_ + 1024
WB_ = M_ + 4096
YT_ = WB_ + 1024
X1_ = 0
FF_ = 4096
MR_ = 15360
F_, QK_, V_ = 4096, 6144, 11264
R1_ = 14336
QT_, KT_, C2_ = 22528, 24576, 27648
QS_ = 28224
JK_ = 4096
AP_, AG_, APT_ = QK_, R1_, R1_ + 2048
MT_ = 6144
M1_ = 4096

BANKS = [[(4, 0), (5, 0), (6, 0), (7, 0)],
         [(0, 1), (1, 2), (2, 3), (3, 4), (4, 5), (5, 6)],
         [(6, 7), (7, 8), (0, 9), (1, 10), (2, 11), (3, 12)]]
STAGED = [96, 77, 96, 88, 80]
PARAMS = 22


def program(nc, a, cst, dft, gmod, gpad, out):
    ctx = ExitStack()
    with ctx:
        def sb(name, shape, dt=F32):
            return ctx.enter_context(nc.sbuf_tensor(name, shape, dt))

        S = {}

        def sem(name):
            if name not in S:
                S[name] = ctx.enter_context(nc.semaphore(name))
            return S[name]

        WH = sb("w_high", [P, 2, 1024], F32R)
        WL = sb("w_low", [P, 2, 1024], F32R)
        AH = sb("act_high", [P, 4, 512], F32R)
        AL = sb("act_low", [P, 4, 512], F32R)
        HH = sb("h_high", [P, KD, T], F32R)
        HL = sb("h_low", [P, KD, T], F32R)
        SH = sb("small_w_high", [P, KD, 32], F32R)
        SL = sb("small_w_low", [P, KD, 32], F32R)
        CD4 = sb("cond_parts", [P, KD, 4], F32R)
        RAW = sb("w_raw", [P, 4, 1024])
        C1 = sb("masks", [P, 512])
        LV = sb("level_masks", [P, 2 * LEVELS, P], mybir.dt.uint8)
        PAR = sb("params", [P, 5, P])
        CW = sb("conv_params", [P, 5 * CH])
        A = sb("arena", [P, ARENA])
        PS = ctx.enter_context(nc.psum_tensor("acc", [P, 8, 512], F32))
        PSF = PS[:, :, :].rearrange("p a b -> p (a b)")
        small_at = [0]
        SM = sb("small", [P, 1600])

        def small(*shape):
            n = int(np.prod(shape))
            v = SM[:, small_at[0]:small_at[0] + n]
            small_at[0] += n
            assert small_at[0] <= 1600
            if len(shape) == 2:
                return v.rearrange("p (a b) -> p a b", b=shape[1])
            if len(shape) == 3:
                return v.rearrange("p (a b c) -> p a b c", b=shape[1], c=shape[2])
            return v

        def arena(at, *shape):
            v = A[:, at:at + int(np.prod(shape))]
            if len(shape) == 2:
                return v.rearrange("p (a b) -> p a b", b=shape[1])
            if len(shape) == 3:
                return v.rearrange("p (a b c) -> p a b c", b=shape[1], c=shape[2])
            return v

        IDN, UPR, ONE, NGM = (C1[:, k * P:(k + 1) * P] for k in range(4))
        FLP = UPR
        FT = arena(FT_, CH, T)
        XN = arena(XN_, NT, D)
        STG = arena(STG_, 5, P)
        LVF = arena(LVL_, 2 * LEVELS * P)
        CT = arena(CT_, 2, T)
        HT = arena(HT_, 2, T)
        WB = arena(WB_, D)
        YT = arena(YT_, D)
        X1 = arena(X1_, NT, D)
        FFT = arena(FF_, FF, T)
        MR = A[0:4, MR_:MR_ + D]

        sumsq = small(18)
        meansq = small(18)
        rstd = small(18)
        half = small(64)
        small_w = arena(HT_ + 1024, KD, 32)
        head_bias = small(24)
        head_log = small(24)
        skip_d = small(HS)
        modT = small(NADA, 2)
        affine = small(3, KD)
        cond = small(KD, 2)
        proj = arena(HT_ + 1280, NT, 32)
        narrow = A[0:32, HT_:HT_ + T]
        sp_x, sp_e, sp_s, sp_q = (arena(SS_ + 96 * i, NT, 24) for i in range(4))
        soft = small(NT, 24)
        nega = small(24)
        logdec = small(NT, 24)
        ncum = small(NT, 24)
        qkg = SM[:, small_at[0]:small_at[0] + 2 * DH]
        ecum = small(NT, 24)
        edec = small(NT, 24)
        etot = small(NT, 24)
        beta = small(NT, H)
        join = SM[0:4, small_at[0]:small_at[0] + 2]
        small_at[0] += 2
        qks = small(NT, 16)
        qkr = small(NT, 16)
        nrk = small(NT, H)
        brk = small(NT, H)
        kbs = small(NT, H)
        kds = small(NT, H)
        rq2 = small(NT, H)
        oss = small(NT, H)
        ors = small(NT, H)
        qkss = small(10, AH_)
        qkrs = small(10, AH_)
        smax = small(AH_ * NT)
        sumsq2 = small(8)
        meansq2 = small(8)
        rstd2 = small(8)
        eps_col = small(1)
        GT_T = arena(YT_, T)
        ssum = small(AH_ * NT)
        srec = small(AH_ * NT)

        w_in = a["w_in"][0]
        w_in_v = w_in.rearrange("(k p) n -> p k n", p=P)
        w_up_v = a["w_up"][0].rearrange("(k p) n -> p k n", p=P)
        w_in2_v = a["w_in_2"][0].rearrange("(k p) n -> p k n", p=P)
        gate_v = a["w_branch_gate_2"][0].rearrange("(k p) n -> p k n", p=P)
        fo_v = a["w_fourier_out_2"][0].rearrange("(k p) n -> p k n", p=P)
        ao_v = a["w_attn_out_2"][0].rearrange("(k p) n -> p k n", p=P)
        mlp1_v = a["w_mlp1_2"][0].rearrange("(k p) n -> p k n", p=P)
        x_rows = a["x"][0].rearrange("(t p) d -> t p d", p=P)
        ctx_rows = a["ctx_2"][0].rearrange("(t p) d -> t p d", p=P)
        out_rows = out[0].rearrange("(t p) d -> t p d", p=P)

        def blocks(eng, n, body, whole=0):
            full = n // 4 - whole
            if full > 1:
                with eng.Fori(0, full) as g:
                    for j in range(4):
                        body(g, j)
            else:
                full = 0
            for g in range(full, (n + 3) // 4):
                for j in range(min(4, n - 4 * g)):
                    body(g, j)

        def up_groups(eng, body):
            with eng.Fori(0, FF // 4) as cg:
                for i in range(4):
                    for j in range(4):
                        body(4 * cg + i, i, j, cg)
            for i in range(FF % 4):
                for j in range(4):
                    body(FF // 4 * 4 + i, i, j, FF // 4)

        def parts(n):
            if n % 4 < 2:
                return [WH[:, n % 2, :], WL[:, n % 2, :]]
            r = slice(2 * (n % 2), 2 * (n % 2) + 2)
            return [v[:, r, :].rearrange("p a b -> p (a b)") for v in (AH, AL)]

        def probs(i):
            return arena(AP_ + (i % 2) * NKEY, NKEY)

        def probs_t(h):
            return arena(APT_ + (h % 2) * 6 * T, 6, T)

        def turned(i):
            b = i % 2
            return PS[:, 4 + 2 * b, :], PS[:, 5, b * CTX:(b + 1) * CTX]

        block = ctx.enter_context(nc.Block())

        def up_to(v, n):
            return v.unsqueeze(2).to_broadcast([P, n, P])

        def each(v, n):
            return v.unsqueeze(1).to_broadcast([P, n, v.shape[1]])

        def as_rows(name, taps=False):
            v = a[name][0]
            return v.rearrange("k (t p) -> (k t) p", p=P) if taps else v.rearrange("(t p) -> t p", p=P)

        parameters = [(STG[0:96, 0, :], as_rows("gdn_conv_w", True)),
                      (STG[0:48, 1, :], as_rows("ssd_conv_w", True)),
                      (STG[48:60, 1, :], as_rows("ssd_conv_b")),
                      (STG[60:68, 1, :], as_rows("pre_mix_norm")),
                      (STG[68:69, 1, :], as_rows("gdn_norm_w")),
                      (STG[69:77, 1, :], as_rows("ssd_norm_w")),
                      (STG[0:88, 2, :], as_rows("ffn_conv_w", True)[0:88, :]),
                      (STG[88:96, 2, :], as_rows("pre_ffn_norm")),
                      (STG[0:44, 3, :], as_rows("ffn_conv_w", True)[88:132, :]),
                      (STG[44:88, 3, :], as_rows("ffn_conv_b")),
                      (STG[0:48, 4, :], as_rows("b_ada_2")),
                      (STG[48:56, 4, :], as_rows("norm1_g_2")),
                      (STG[56:64, 4, :], as_rows("norm2_g_2")),
                      (STG[64:72, 4, :], as_rows("c_2")),
                      (STG[72:80, 4, :], a["c_ctx_2"].rearrange("(t p) -> t p", p=P)),
                      (small_w[:, :, 0:16], w_in_v[:, :, 4096:4112]),
                      (small_w[:, :, 16:32], w_in_v[:, :, 6672:6688]),
                      (head_bias[:, 0:8], a["gdn_dt_bias"].to_broadcast([P, 8])),
                      (head_bias[:, 8:24], a["ssd_dt_bias"].to_broadcast([P, HS])),
                      (head_log[:, 0:8], a["gdn_a_log"].to_broadcast([P, 8])),
                      (head_log[:, 8:24], a["ssd_a_log"].to_broadcast([P, HS])),
                      (skip_d, a["ssd_d"].to_broadcast([P, HS]))]

        @block.sync
        def _(sp):
            for t in range(NT):
                sp.dma_start(XN[:, t, :], x_rows[t]).then_inc(sem(f"x_in{t}"), 16)

            for dst, src in parameters[PARAMS // 2:]:
                sp.dma_start(dst, src).then_inc(sem("params_in"), 16)

            def load(g, off, src, shape):
                sp.wait_ge(sem("w_low"), 4 * g + off + 1)
                dst = RAW[:, off % 4, :]
                if shape is not None:
                    dst = dst.rearrange("p (k c) -> p k c", c=shape)
                sp.dma_start(dst, src).then_inc(sem(f"w_in{off % 4}"), 16)

            def columns(n0, first, view, w=P):
                def body(g, j):
                    load(g, n0 + j, view[:, :, ds(first + g * (4 * w) + j * w, w)], w)
                return body

            def rows(n0, view):
                v = view.rearrange("(k p) n -> k p n", p=P)

                def body(g, j):
                    load(g, n0 + j, v[4 * g + j], None)
                return body

            blocks(sp, X0, columns(CONV_N, 0, w_in_v))
            blocks(sp, CH - X0, columns(CONV_N + X0, 5136, w_in_v))
            blocks(sp, 8, columns(Z_N, 4112, w_in_v))
            blocks(sp, 8, columns(Z_N + 8, 3072, w_in_v))
            blocks(sp, 16, rows(WO_N, a["w_out"][0]))

            ada_rows = a["w_ada_2"][0]

            def up(q, i, j, cg):
                if j < 2:
                    load(q, UP_N + j, w_up_v[:, :, ds(q * P + j * (FF * P), P)], P)
                else:
                    k = 2 * i + j - 2
                    load(q, UP_N + j, ada_rows[k * P:(k + 1) * P, ds(cg * D, D)], None)

            up_groups(sp, up)
            for j in range(4):
                load(0, UP_N + 4 * FF + j, ada_rows[(4 + j) * P:(5 + j) * P, 5 * D:6 * D], None)
            blocks(sp, FF, rows(DN_N, a["w_down"][0]))
            blocks(sp, 4, columns(PR_N, 0, w_in2_v))
            for part in range(3):
                for j in range(4):
                    load(0, PR_N + 4 + 4 * part + j,
                         w_in2_v[:, 2 * j:2 * j + 2, 512 * (part + 1):512 * (part + 2)], 512)
            blocks(sp, 16, columns(GT_N, 0, gate_v))
            for b in range(4):
                load(0, FA_N + 2 * b, fo_v[:, :, 256 * b:256 * (b + 1)], 256)
                load(0, FA_N + 2 * b + 1, ao_v[:, :, 256 * b:256 * (b + 1)], 256)
            blocks(sp, 8, rows(W2_N, a["w_out_2"][0]))
            blocks(sp, MF, columns(M1_N, 0, mlp1_v))
            blocks(sp, MF, rows(M2_N, a["w_mlp2_2"][0]))
            for t in range(NT):
                sp.wait_ge(sem("x_res"), 3 * NT + t + 1)
                sp.dma_start(out_rows[t], X1[:, t, :]).then_inc(sem("stored"), 16)
            sp.wait_ge(sem("stored"), 16 * NT)

        @block.tensor
        def _(pe):
            def products(out_, wh, wl, xh, xl, start, stop):
                pe.matmul(out_, wh, xh, start=start, stop=False)
                pe.matmul(out_, wh, xl, start=False, stop=False)
                return pe.matmul(out_, wl, xh, start=False, stop=stop)

            def split_ready(g, off):
                pe.wait_ge(sem("w_low"), 4 * g + off + 1 + 4)

            def column_block(g, off, bank, xh, xl, n=T, first=None):
                split_ready(g, off)
                s = off % 2
                for k in range(KD):
                    if first is not None:
                        pe.wait_ge(sem("n_low"), first + k + 1)
                    c = slice(k * P, (k + 1) * P)
                    m = products(PS[:, bank, 0:n], WH[:, s, c], WL[:, s, c], xh[:, k, :], xl[:, k, :],
                                 k == 0, k == KD - 1)
                m.then_inc(sem("w_used"), 1)

            def row_block(g, off, j, a0, k_is_0, k_is_last, freed=()):
                split_ready(g, off)
                pe.wait_ge(sem("a_low"), a0 + 4 * g + j + 1)
                s, r = off % 2, (a0 + j) % 4
                for t in range(NT):
                    if t < len(freed):
                        pe.wait_ge(sem(freed[t][0]), freed[t][1])
                    tc = slice(t * P, (t + 1) * P)
                    for f in range(2):
                        fc = slice(f * 512, (f + 1) * 512)
                        o = PS[:, 2 * t + f, :]
                        pe.matmul(o, AH[:, r, tc], WH[:, s, fc], start=k_is_0, stop=False)
                        pe.matmul(o, AH[:, r, tc], WL[:, s, fc], start=False, stop=False)
                        m = pe.matmul(o, AL[:, r, tc], WH[:, s, fc], start=False, stop=k_is_last)
                    if k_is_last and t < NT - 1:
                        m.then_inc(sem("rows_done"), 1)
                m.then_inc(sem("w_used"), 1)

            def down(n0, a0, n, freed=()):
                def body(g, j, first=False, last=False):
                    row_block(g, n0 + j, j, a0, first and j == 0, last, freed if first and j == 0 else ())
                for j in range(4):
                    body(0, j, first=True)
                full = n // 4
                mid_end = full if n % 4 else full - 1
                if mid_end > 2:
                    with pe.Fori(1, mid_end) as g:
                        for j in range(4):
                            body(g, j)
                else:
                    for g in range(1, mid_end):
                        for j in range(4):
                            body(g, j)
                for g in range(mid_end, (n + 3) // 4):
                    for j in range(min(4, n - 4 * g)):
                        body(g, j, last=4 * g + j == n - 1)

            def turn(job, x, nt, tiles):
                pe.wait_ge(sem("n_x"), tiles + nt)
                for k in range(KD):
                    if 8 * job + k > 3:
                        pe.wait_ge(sem("n_low"), 8 * job + k - 3)
                    for t in range(nt):
                        m = pe.transpose(PS[:, 4 + k % 4, t * P:(t + 1) * P],
                                         x[:, t, k * P:(k + 1) * P], IDN)
                    m.then_inc(sem("n_turned"), 1)

            pe.wait_ge(sem("consts_in"), 16)
            pe.wait_ge(sem("params_in"), PARAMS * 16)
            for s, r in enumerate(STAGED):
                m = pe.transpose(PS[:, s // 4, (s % 4) * P:(s % 4) * P + r], STG[0:r, s, :],
                                 IDN[0:r, 0:r])
            m.then_inc(sem("params_turned"), 1)
            turn(0, XN, NT, 0)
            pe.wait_ge(sem("params_out"), 5)

            def sum_squares(g, j):
                pe.wait_ge(sem("qk_square"), 4 * g + j + 1)
                for c in range(NT):
                    m = pe.matmul(PS[:, 6, ds(2 * (c * 16 + j) + 8 * g, 2)],
                                  arena(QE_ + (j % 4) * T, T)[:, c * P:(c + 1) * P],
                                  ONE[:, 0:2], start=True, stop=True)
                m.then_inc(sem("qk_sum"), 1)

            def conv(g, j):
                pe.wait_ge(sem("conv_step"), 3 * (4 * g + j) + 3)
                column_block(g, CONV_N + j, j, HH, HL,
                             first=0 if isinstance(g, int) and g == 0 else None)

            def conv_qk(g, j):
                conv(g, j)
                if j > 1 or not isinstance(g, int) or g:
                    sum_squares(g, j - 2)

            for j in range(4):
                conv_qk(0, j)
            pe.wait_ge(sem("small_low"), 1)
            for k in range(KD):
                m = products(PS[0:32, 7, :], SH[:, k, :], SL[:, k, :], HH[:, k, :], HL[:, k, :],
                             k == 0, k == KD - 1)
            m.then_inc(sem("narrow_done"), 1)
            pe.wait_ge(sem("narrow_out"), 1)
            for t in range(NT):
                m = pe.transpose(PS[:, 7, t * 32:(t + 1) * 32], narrow[:, t * P:(t + 1) * P],
                                 IDN[0:32, 0:32])
            m.then_inc(sem("proj_done"), 1)
            with pe.Fori(1, 4) as g:
                for j in range(4):
                    conv_qk(g, j)
            for j in range(4):
                conv(4, j)
                if j < 2:
                    sum_squares(4, j - 2)
            pe.wait_ge(sem("logdec_ready"), 1)
            pe.matmul(PS[:, 4, 0:96], UPR, logdec.rearrange("p a b -> p (a b)"), start=True, stop=True)
            pe.matmul(PS[:, 5, 0:96], ONE, logdec.rearrange("p a b -> p (a b)"), start=True, stop=True)\
                .then_inc(sem("cum_done"), 1)
            with pe.Fori(5, CH // 4) as g:
                for j in range(4):
                    conv(g, j)
            pe.wait_ge(sem("conv_step"), 12 + 3 * (CH - 2))

            def four(q):
                return range(4 * q, 4 * q + 4)

            for c in range(NT):
                tc = slice(c * P, (c + 1) * P)

                def tile(at, h):
                    return arena(at + h * P, P)

                for q in range(2):
                    for h in four(q):
                        m = pe.matmul(PS[:, q, (h % 4) * P:(h % 4 + 1) * P],
                                      logdec[:, c, h:h + 1].to_broadcast([P, P]), UPR,
                                      start=True, stop=True)
                    m.then_inc(sem("d_cum"), 1)
                if c:
                    pe.wait_ge(sem("y_turned_out"), 2 * c)
                else:
                    pe.wait_ge(sem("scales_ready"), 1)
                    pe.wait_ge(sem("cum_exp"), 3)
                    pe.wait_ge(sem("conv_out"), CH)
                for q in range(2):
                    for h in four(q):
                        pe.matmul(PS[:, 2 + q, (h % 4) * P:(h % 4 + 1) * P],
                                  brk[:, c, h:h + 1].to_broadcast([P, P]), IDN, start=True, stop=True)
                    for h in four(q):
                        pe.matmul(PS[:, 4 + q, (h % 4) * P:(h % 4 + 1) * P], FT[:, K0 + h, tc],
                                  FT[:, K0 + h, tc], start=True, stop=True)
                    for h in four(q):
                        m = pe.matmul(PS[:, 6 + q, (h % 4) * P:(h % 4 + 1) * P], FT[:, K0 + h, tc],
                                      FT[:, Q0 + h, tc], start=True, stop=True)
                    m.then_inc(sem("d_gram"), 1)
                for q in range(2):
                    pe.wait_ge(sem("d_r0"), 2 * c + q + 1)
                    for h in four(q):
                        m = pe.transpose(PS[:, q, (h % 4) * P:(h % 4 + 1) * P], tile(R_, h), IDN)
                    m.then_inc(sem("d_r0_turned"), 1)
                for level in range(1, LEVELS):
                    u = 2 * (c * (LEVELS - 1) + level - 1) + 1
                    for q in range(2):
                        pe.wait_ge(sem("d_level"), 2 * (c * LEVELS + level - 1) + q + 1)
                        for h in four(q):
                            m = pe.matmul(PS[:, 2 + q, (h % 4) * P:(h % 4 + 1) * P], tile(NM_, h),
                                          tile(TT_, h), start=True, stop=True)
                        m.then_inc(sem("d_nt"), 1)
                    for q in range(2):
                        pe.wait_ge(sem("d_nt_out"), u + q)
                        if level < LEVELS - 1:
                            for h in four(q):
                                pe.matmul(PS[:, 4 + q, (h % 4) * P:(h % 4 + 1) * P], tile(R_, h),
                                          tile(PP_, h), start=True, stop=True)
                        for h in four(q):
                            m = pe.matmul(PS[:, 6 + q, (h % 4) * P:(h % 4 + 1) * P], tile(PP_, h),
                                          tile(R_, h), start=True, stop=True)
                        m.then_inc(sem("d_tnt"), 1)
                for q in range(2):
                    for h in four(q):
                        pe.transpose(PS[:, q, (h % 4) * P:(h % 4 + 1) * P], FT[:, K0 + h, tc], IDN)
                    for h in four(q):
                        m = pe.transpose(PS[:, 2 + q, (h % 4) * P:(h % 4 + 1) * P], FT[:, V0 + h, tc], IDN)
                    m.then_inc(sem("d_kv_turned"), 1)
                for q in range(2):
                    pe.wait_ge(sem("d_kv_out"), 2 * c + q + 1)
                    for h in four(q):
                        m = pe.matmul(PS[:, 4 + q, (h % 4) * P:(h % 4 + 1) * P], tile(TT_, h),
                                      tile(R_, h), start=True, stop=True)
                    m.then_inc(sem("d_w"), 1)
                for q in range(2):
                    pe.wait_ge(sem("d_w_out"), 2 * c + q + 1)
                    for h in four(q):
                        o = PS[:, 6 + q, (h % 4) * P:(h % 4 + 1) * P]
                        m = pe.matmul(o, tile(R_, h), tile(PP_, h), start=True, stop=c == 0)
                        if c:
                            m = pe.matmul(o, tile(NW_, h), tile(SD_, h), start=False, stop=True)
                    m.then_inc(sem("d_new"), 1)
                    if c:
                        for h in four(q):
                            m = pe.matmul(PS[:, q, (h % 4) * P:(h % 4 + 1) * P], FT[:, Q0 + h, tc],
                                          tile(SD_, h), start=True, stop=True)
                        m.then_inc(sem("d_qs"), 1)
                for q in range(2):
                    pe.wait_ge(sem("d_new_out"), 2 * c + q + 1)
                    for h in four(q):
                        pe.matmul(PS[:, 2 + q, (h % 4) * P:(h % 4 + 1) * P], tile(QE_, h),
                                  tile(VN_, h), start=True, stop=True)
                    for h in four(q):
                        m = pe.matmul(PS[:, 4 + q, (h % 4) * P:(h % 4 + 1) * P], tile(NM_, h),
                                      tile(VN_, h), start=True, stop=True)
                    m.then_inc(sem("d_out"), 1)
                pe.wait_ge(sem("d_state"), 2 * c + 2)
                for i in range(8):
                    pe.transpose(PS[:, i // 4, (i % 4) * P:(i % 4 + 1) * P], FT[:, X0 + i, tc], IDN)
                for g in range(2):
                    m = pe.transpose(PS[:, 2, g * P:(g + 1) * P], FT[:, B0 + g, tc], IDN)
                m.then_inc(sem("s_turned"), 1)
                for g in range(2):
                    pe.matmul(PS[:, 3, g * P:(g + 1) * P], FT[:, B0 + g, tc], FT[:, C0 + g, tc],
                              start=True, stop=True)

                def cumulated(g):
                    for h in range(8):
                        m = pe.matmul(PS[:, 4 + 2 * g + h // 4, (h % 4) * P:(h % 4 + 1) * P],
                                      logdec[:, c, 8 + 8 * g + h:9 + 8 * g + h].to_broadcast([P, P]),
                                      UPR, start=True, stop=True)
                    m.then_inc(sem("s_cum"), 1)

                cumulated(0)
                for q in range(2):
                    pe.wait_ge(sem("d_normed"), 2 * c + q + 1)
                    for h in four(q):
                        m = pe.transpose(PS[:, 6 + q, (h % 4) * P:(h % 4 + 1) * P], tile(R_, h), IDN)
                    m.then_inc(sem("d_o_turned"), 1)
                pe.wait_ge(sem("d_o_out"), 2 * c + 2)
                cumulated(1)
                for g in range(2):
                    pe.wait_ge(sem("s_m"), 2 * c + g + 1)
                    for h in range(8):
                        pe.matmul(PS[:, 4 + 2 * g, h * PD:(h + 1) * PD], tile([QE_, R_][g], h),
                                  arena(TT_ + (8 * g + h) * PD, PD), start=True, stop=True)
                    if c:
                        pe.matmul(PS[:, 5 + 2 * g, :], FT[:, C0 + g, tc], arena(SS_ + g * 512, 512),
                                  start=True, stop=True)
                    if g == 0:
                        pe.wait_ge(sem("s_b_out"), c + 1)
                    pe.matmul(PS[:, g, :], arena(NW_ + g * P, P), arena(NM_ + g * 512, 512),
                              start=True, stop=True).then_inc(sem("s_sum"), 1)
                for g in range(2):
                    pe.wait_ge(sem("s_y"), 2 * c + g + 1)
                    for i in range(4):
                        m = pe.transpose(PS[:, 2 + g, i * P:(i + 1) * P],
                                         arena(VN_ + g * 512 + i * P, P), IDN)
                    m.then_inc(sem("y_turned"), 1)
            pe.wait_ge(sem("y_turned_out"), 2 * NT)

            def gated(g, j):
                pe.wait_ge(sem("z_step"), 4 * g + j + 1)
                column_block(g, Z_N + j, j, HH, HL)

            for i in range(12):
                gated(i // 4, i % 4)
            for g in range(2):
                for i in range(4):
                    pe.wait_ge(sem("y_square"), 4 * g + i + 1)
                    m = pe.matmul(PS[:, 4 + g, :], ONE, arena(NM_ + (4 * g + i) * T, T),
                                  start=i == 0, stop=i == 3)
                    m.then_inc(sem("y_sum"), 1)
            for j in range(4):
                gated(3, j)
            pe.wait_ge(sem("y_ln"), 4)
            pe.wait_ge(sem("z_silu"), 16)
            down(WO_N, WO_A, 16)
            turn(1, XN, NT, 4)

            def modulation(q, j, k):
                split_ready(q, UP_N + j)
                wh, wl = parts(j)
                for v in range(2):
                    vc = slice(v * 512, (v + 1) * 512)
                    pe.matmul(PS[0:4, 4 + v, :], CD4[:, k, :], wh[:, vc], start=k == 0, stop=False)
                    m = pe.matmul(PS[0:4, 4 + v, :], CD4[:, k, :], wl[:, vc], start=False,
                                  stop=k == KD - 1)
                m.then_inc(sem("w_used"), 1)

            def ffn(q, i, j, cg):
                if j < 2:
                    pe.wait_ge(sem("ffn_step"), 5 * q + [2, 4][j])
                    column_block(q, UP_N + j, j, HH, HL)
                else:
                    if i == 0 and j == 2:
                        turn_rows(cg)
                    modulation(q, j, 2 * i + j - 2)

            def turn_rows(cg):
                pe.wait_ge(sem("mod_rows"), cg + 1)
                for i in range(KD):
                    m = pe.matmul(PS[:, 6, ds(cg * (2 * KD) + 2 * i, 2)], MR[:, i * P:(i + 1) * P],
                                  join, start=True, stop=True)
                m.then_inc(sem("mod_turned"), 1)

            pe.wait_ge(sem("n_low"), 16)
            pe.wait_ge(sem("join_ready"), 1)
            up_groups(pe, ffn)
            for j in range(4):
                modulation(FF, j, 4 + j)
            turn_rows(6)
            down(DN_N, DN_A, FF, [("ffn_step", 5 * FF + 5), ("ffn_step", 5 * FF + 5), ("mod_rows", 7),
                                  ("mod_out", 1)])
            turn(2, XN, NT, 8)
            turn(3, arena(QT_, 2, D), 2, 12)
            for j in range(4):
                column_block(0, PR_N + j, j, HH, HL, first=16 if j == 0 else None)
            pe.wait_ge(sem("n_low"), 32)
            XH = AH[:, :, :].rearrange("p a b -> p (a b)").rearrange("p (k t) -> p k t", t=CTX)
            XL = AL[:, :, :].rearrange("p a b -> p (a b)").rearrange("p (k t) -> p k t", t=CTX)
            for part in range(3):
                for b in range(4):
                    n = PR_N + 4 + 4 * part + b
                    split_ready(0, n)
                    for i in range(4 if part == 0 else 6):
                        bank, free = BANKS[part][i]
                        if b == 0 and free:
                            pe.wait_ge(sem("pr_out"), free)
                        for kk in range(2):
                            k = 2 * b + kk
                            if i < 4:
                                xh, xl = HH[:, k, i * P:(i + 1) * P], HL[:, k, i * P:(i + 1) * P]
                            else:
                                xh, xl = XH[:, k, (i - 4) * P:(i - 3) * P], XL[:, k, (i - 4) * P:(i - 3) * P]
                            wc = slice(kk * 512, (kk + 1) * 512)
                            o = PS[:, bank, :]
                            pe.matmul(o, xh, WH[:, n % 2, wc], start=k == 0, stop=False)
                            pe.matmul(o, xh, WL[:, n % 2, wc], start=False, stop=False)
                            m = pe.matmul(o, xl, WH[:, n % 2, wc], start=False, stop=k == KD - 1)
                    m.then_inc(sem("w_used"), 1)
            CD = arena(C2_ + GRID, 2 * P)
            V12 = arena(R1_, NT, 4, 2 * P)
            CSN = arena(R1_ + 4096, 2, NT, T)
            pe.wait_ge(sem("pr_out"), 20)
            pe.wait_ge(sem("dft_in"), 32)
            for t in range(NT):
                for u in range(2):
                    for gr in range(2 * u, 2 * u + 2):
                        m = pe.matmul(PS[:, 2 * (t % 2) + u, (gr % 2) * 256:(gr % 2 + 1) * 256],
                                      arena(F_ + gr * T + t * P, P), CD, start=True, stop=True)
                    m.then_inc(sem("f_mix"), 1)
                if t:
                    pe.wait_ge(sem("f_mix_out"), 2 * t)
            pe.wait_ge(sem("f_mix_out"), 8)
            for gr in range(4):
                for kt in range(NT):
                    for v in range(2):
                        m = pe.matmul(PS[:, 4 + gr, :], V12[:, kt, gr, v * P:(v + 1) * P],
                                      CSN[:, v, kt, :], start=kt == 0 and v == 0,
                                      stop=kt == NT - 1 and v == 1)
                m.then_inc(sem("f_done"), 1)
            QKt = arena(QK_, 10, 4, P)
            for i in range(10):
                pe.wait_ge(sem("qk_ready"), i + 1)
                if i > 3:
                    pe.wait_ge(sem("qk_turned_out"), i - 3)
                for f in range(4):
                    m = pe.transpose(PS[:, i % 4, f * P:(f + 1) * P], QKt[:, i, f, :], IDN)
                m.then_inc(sem("qk_turned"), 1)
            QT = arena(QT_, 4, T)
            KT = arena(KT_, 4, NKEY)
            V = arena(V_, 6, T)
            pe.wait_ge(sem("qk_turned_out"), 10)
            pe.wait_ge(sem("f_out"), 4)

            def scores(i):
                h, t = divmod(i, NT)
                r = slice(DH * (h % 2), DH * (h % 2) + DH)
                if i > 1:
                    pe.wait_ge(sem("at_exp"), i - 1)
                pe.wait_ge(sem("bias_ready"), h + 1)
                pe.matmul(PS[:, 2 * (i % 2), :], FLP,
                          arena(AG_ + (h % 2) * 1024 + (7 - 2 * t) * GRID, T), start=True, stop=False)
                pe.matmul(PS[:, 2 * (i % 2), :], QT[r, h // 2, t * P:(t + 1) * P], KT[r, h // 2, 0:T],
                          start=False, stop=True)
                pe.matmul(PS[:, 2 * (i % 2) + 1, 0:CTX], QT[r, h // 2, t * P:(t + 1) * P],
                          KT[r, h // 2, T:NKEY], start=True, stop=True).then_inc(sem("at_scores"), 1)

            def values(h):
                pe.wait_ge(sem("at_main_out"), NT * (h + 1))
                pe.wait_ge(sem("at_ctx_out"), NT * (h + 1))
                if h:
                    pe.wait_ge(sem("at_o_out"), h)
                r = slice(DH * (h % 2), DH * (h % 2) + DH)
                for kt in range(6):
                    m = pe.matmul(PS[r, 7, :], V[:, kt, h * DH:(h + 1) * DH], probs_t(h)[:, kt, :],
                                  start=kt == 0, stop=kt == 5)
                m.then_inc(sem("at_o"), 1)

            scores(0)
            for i in range(AH_ * NT):
                if i + 1 < AH_ * NT:
                    scores(i + 1)
                pe.wait_ge(sem("at_scaled"), i + 1)
                if i > 1:
                    pe.wait_ge(sem("at_main_out"), i - 1)
                main, side = turned(i)
                for kt in range(6):
                    if kt == 4 and i:
                        pe.wait_ge(sem("at_ctx_out"), i)
                    o = main[:, kt * P:(kt + 1) * P] if kt < 4 else side[:, (kt - 4) * P:(kt - 3) * P]
                    m = pe.transpose(o, probs(i)[:, kt * P:(kt + 1) * P], IDN)
                m.then_inc(sem("at_p_turned"), 1)
                if i and i % NT == 0:
                    values(i // NT - 1)
            values(AH_ - 1)

            def gate(g, j):
                pe.wait_ge(sem("gate_out"), 4 * g + j + 1)
                column_block(g, GT_N + j, j, HH, HL)

            blocks(pe, 16, gate)
            pe.wait_ge(sem("gate_out"), 20)
            for b in range(4):
                for v in range(2):
                    n = FA_N + 2 * b + v
                    split_ready(0, n)
                    if b == 0:
                        pe.wait_ge(sem("branch_low"), 4 * (v + 1))
                    for mm in range(2):
                        if v == 0 and b > 1:
                            pe.wait_ge(sem("merge_out"), 2 * b + mm - 3)
                        for k in range(4):
                            wc = slice(k * 256 + mm * P, k * 256 + mm * P + P)
                            xh = HH[:, k, :] if v else AH[:, k, :]
                            xl = HL[:, k, :] if v else AL[:, k, :]
                            m = products(PS[:, 4 * (b % 2) + 2 * mm + v, :], WH[:, n % 2, wc], WL[:, n % 2, wc],
                                         xh, xl, k == 0, k == 3)
                    m.then_inc(sem("w_used"), 1)
            down(W2_N, W2_A, 8, [("merge_out", 5 + t) for t in range(NT)])
            turn(4, XN, NT, 14)

            def mlp(g, j):
                pe.wait_ge(sem("mlp_out"), 4 * g + j + 1)
                column_block(g, M1_N + j, j, HH, HL,
                             first=32 if isinstance(g, int) and g == 0 and j == 0 else None)

            for j in range(4):
                mlp(0, j)
            with pe.Fori(1, MF // 4) as g:
                for j in range(4):
                    mlp(g, j)
            down(M2_N, M2_A, MF, [("mlp_relu", MF - 2), ("mlp_relu", MF)])

        @block.scalar
        def _(act):
            f = act.activation
            act.dma_start(C1[:, :], cst[:, 0:512]).then_inc(sem("consts_in"), 16)
            def split(g, off):
                act.wait_ge(sem(f"w_in{off % 4}"), 16 * g + 16 * (off // 4 + 1))
                act.wait_ge(sem("w_used"), 4 * g + off + 1)
                f(WH[:, off % 2, :], RAW[:, off % 4, :], ACT.Copy).then_inc(sem("w_high"), 1)

            def used(g, off):
                act.wait_ge(sem("w_used"), 4 * g + off + 1 + 2)

            def act_split(g, j, a0, n0, src):
                act.wait_ge(sem("w_used"), 4 * g + j + n0 - 4 + 1 + 2)
                f(AH[:, (a0 + j) % 4, :], src[:, 4 * g + j, :], ACT.Copy).then_inc(sem("a_high"), 1)

            def norm(job, x, nt, tiles, ready, first=0):
                for t in range(first, first + nt):
                    if len(ready) == 2:
                        act.wait_ge(sem(ready[0]), ready[1] + t)
                    else:
                        act.wait_ge(sem(f"{ready[0]}{t}"), 16)
                    junk = arena(JK_, NT, D) if job in (0, 3) else XN
                    f(junk[:, t, :], x[:, t, :], ACT.Square,
                      accum_out=sumsq[:, tiles + t:tiles + t + 1]).then_inc(sem("n_square"), 1)

            def norm_high(job, nt, gain=None, shift=None):
                hh = HH if job != 3 else AH[:, :, :].rearrange("p a b -> p (a b)")\
                    .rearrange("p (k t) -> p k t", t=CTX)
                for k in range(KD):
                    src = PS[:, 4 + k % 4, 0:nt * P]
                    if shift is None:
                        act.wait_ge(sem("n_turned"), 8 * job + k + 1)
                        f(hh[:, k, :], src, ACT.Copy, scale=gain(k)).then_inc(sem("n_high"), 1)
                        continue
                    if k % 2:
                        act.wait_ge(sem("n_turned"), 8 * job + k + 1)
                        act.wait_ge(sem("n_low"), 8 * job + k - 1)
                        f(HT[:, 1, 0:nt * P], src, ACT.Identity, scale=gain(k), bias=shift(k))\
                            .then_inc(sem("n_odd"), 1)
                        act.wait_ge(sem("n_odd"), 4 * (job - 2) + k // 2 + 1)
                    else:
                        act.wait_ge(sem("n_even"), 4 * (job - 2) + k // 2 + 1)
                    f(hh[:, k, :], HT[:, k % 2, 0:nt * P], ACT.Copy).then_inc(sem("n_high"), 1)

            def down(n0, a0, n, src, ready, begun=0):
                for j in range(begun, 2):
                    act.wait_ge(sem(ready[0]), ready[1](j))
                    act_split(0, j, a0, n0, src)

                def body(g, j):
                    if not isinstance(g, int) or 4 * g + j + 2 < n:
                        act.wait_ge(sem(ready[0]), ready[1](4 * g + j + 2))
                        act_split(g + (j + 2) // 4, (j + 2) % 4, a0, n0, src)
                    if not isinstance(g, int) or (4 * g + j + 1 < n and n0 + 4 * g + j + 2 < END_N):
                        split(g, n0 + j + 2)

                blocks(act, n, body, whole=1)

            act.preload_act_table_set("silu_and_others")
            for i, (dst, src) in enumerate(parameters[:PARAMS // 2]):
                act.dma_start(dst, src).then_inc(sem("params_in"), 16)
                if i % 3 == 2:
                    norm(0, XN, 1, 0, ("x_in",), i // 3)
            norm(0, XN, NT - PARAMS // 6, 0, ("x_in",), PARAMS // 6)
            act.dma_start(LVF, cst[:, LEVEL:COLMASK]).then_inc(sem("levels_raw"), 16)
            act.wait_ge(sem("params_out"), 5)
            f(cond[:, :, 0], PAR[:, 4, 64:72], ACT.Silu).then_inc(sem("cond"), 1)
            f(cond[:, :, 1], PAR[:, 4, 72:80], ACT.Silu).then_inc(sem("cond"), 1)
            act.wait_ge(sem("cond"), 2)
            f(CD4[:, :, 0:2], cond, ACT.Copy).then_inc(sem("small_high"), 1)
            f(SH[:, :, :], small_w, ACT.Copy).then_inc(sem("small_high"), 1)
            split(0, 0)
            split(0, 1)
            norm_high(0, NT, lambda k: PAR[:, 1, 60 + k:61 + k])

            def conv(g, j):
                i = 4 * g + j
                split(g, CONV_N + j + 2)
                used(g, CONV_N + j)
                f(CT[:, j % 2, :], PS[:, j, :], ACT.Copy, scale=CW[:, ds(3 * CH + i, 1)])\
                    .then_inc(sem("tap"), 1)
                act.wait_ge(sem("conv_step"), 12 + 3 * i + 3)
                f(FT[:, i, :], CT[:, j % 2, :], ACT.Silu, bias=CW[:, ds(4 * CH + i, 1)])\
                    .then_inc(sem("conv_out"), 1)

            for j in range(4):
                conv(0, j)
            act.wait_ge(sem("narrow_done"), 1)
            f(narrow, PS[0:32, 7, :], ACT.Copy).then_inc(sem("narrow_out"), 1)
            for j in range(4):
                conv(1, j)
            act.preload_act_table_set("exp_and_others")
            act.wait_ge(sem("sp_abs"), 1)
            f(sp_e, sp_e, ACT.Exp, scale=-1.0).then_inc(sem("sp_exp"), 1)
            f(nega, head_log, ACT.Exp).then_inc(sem("sp_exp"), 1)
            f(beta, proj[:, :, 0:8], ACT.Exp, scale=-1.0).then_inc(sem("sp_exp"), 1)
            act.preload_act_table_set("silu_and_others")
            with act.Fori(2, 4) as g:
                for j in range(4):
                    conv(g, j)
            with act.Fori(4, 6) as g:
                for j in range(4):
                    conv(g, j)
            act.preload_act_table_set("exp_and_others")
            act.wait_ge(sem("cum_out"), 1)
            f(ecum, ncum, ACT.Exp, scale=-1.0).then_inc(sem("cum_exp"), 1)
            f(edec, edec, ACT.Exp).then_inc(sem("cum_exp"), 1)
            f(etot, PS[:, 5, 0:96].rearrange("p (a b) -> p a b", b=24), ACT.Exp).then_inc(sem("cum_exp"), 1)
            act.preload_act_table_set("silu_and_others")
            with act.Fori(6, CH // 4) as g:
                for j in range(4):
                    conv(g, j)
            act.preload_act_table_set("exp_and_others")

            def four(q):
                return range(4 * q, 4 * q + 4)

            def tiles(at, q):
                return arena(at + q * 512, 512)

            for c in range(NT):
                tc = slice(c * P, (c + 1) * P)
                for q in range(2):
                    act.wait_ge(sem("d_arg"), 2 * c + q + 1)
                    for h in four(q):
                        m = f(arena(PP_ + h * P, P), arena(PP_ + h * P, P), ACT.Exp,
                              bias=ncum[:, c, h:h + 1])
                    m.then_inc(sem("d_exp"), 1)
                for level in range(1, LEVELS):
                    u = 2 * (c * (LEVELS - 1) + level - 1) + 1
                    for q in range(2):
                        act.wait_ge(sem("d_nt"), u + q)
                        if level == 1:
                            act.wait_ge(sem("d_level"), 2 * c * LEVELS + 2)
                        else:
                            act.wait_ge(sem("d_tnt"), u - 2 + q)
                        f(tiles(PP_, q), PS[:, 2 + q, :], ACT.Copy).then_inc(sem("d_nt_out"), 1)
                for q in range(2):
                    act.wait_ge(sem("d_w"), 2 * c + q + 1)
                    f(tiles(NW_, q), PS[:, 4 + q, :], ACT.Copy, scale=-1.0).then_inc(sem("d_w_out"), 1)
                for q in range(2):
                    act.wait_ge(sem("d_new"), 2 * c + q + 1)
                    f(tiles(VN_, q), PS[:, 6 + q, :], ACT.Copy).then_inc(sem("d_new_out"), 1)
                for q in range(2):
                    act.wait_ge(sem("d_o"), 2 * c + q + 1)
                    f(tiles(PP_, q), tiles(R_, q), ACT.Square).then_inc(sem("d_o_square"), 1)
                act.wait_ge(sem("s_turned"), c + 1)
                f(arena(NW_, 2 * P), PS[:, 2, 0:2 * P], ACT.Copy).then_inc(sem("s_b_out"), 1)
                for q in range(2):
                    act.wait_ge(sem("d_o_turned"), 2 * c + q + 1)
                    f(FT[:, Q0 + 4 * q:Q0 + 4 * q + 4, tc], PS[:, 6 + q, :].rearrange("p (h t) -> p h t", t=P),
                      ACT.Copy, scale=PAR[:, 1, 68:69]).then_inc(sem("d_o_out"), 1)
                for g in range(2):
                    act.wait_ge(sem("s_arg"), 2 * c + g + 1)
                    for h in range(8):
                        m = f(arena([QE_, R_][g] + h * P, P), arena([QE_, R_][g] + h * P, P), ACT.Exp,
                              bias=ncum[:, c, 8 + 8 * g + h:9 + 8 * g + h])
                    m.then_inc(sem("s_exp"), 1)
                for g in range(2):
                    act.wait_ge(sem("y_turned"), 2 * c + g + 1)
                    f(FT[:, X0 + 4 * g:X0 + 4 * g + 4, tc], PS[:, 2 + g, :].rearrange("p (h t) -> p h t", t=P),
                      ACT.Copy).then_inc(sem("y_turned_out"), 1)
            act.preload_act_table_set("silu_and_others")

            def gated(g, j):
                last = 4 * g + j == 15
                if not last:
                    split(g, Z_N + j + 2)
                used(g, Z_N + j)
                act.wait_ge(sem("z_step"), 4 * g + j + 1)
                f(arena(R_ + j * T, T), PS[:, j, :], ACT.Silu).then_inc(sem("z_silu"), 1)
                if last:
                    split(0, WO_N + 1)

            def gated_s(g, j):
                gated(g, j)
                i = 4 * g + j
                act.wait_ge(sem("z_step"), i + 5)
                f(arena(NM_ + i * T, T), FT[:, X0 + i, :], ACT.Square).then_inc(sem("y_square"), 1)

            for g in range(2):
                for j in range(4):
                    gated_s(g, j)
            for j in range(4):
                gated(2, j)
            act.preload_act_table_set("natural_log_exp_and_others")
            for g in range(2):
                act.wait_ge(sem("y_sum"), 4 * g + 4)
                f(arena(QE_ + g * T, T), PS[:, 4 + g, :], ACT.Ln, scale=1.0 / 512, bias=eps_col)\
                    .then_inc(sem("y_ln"), 1)
                act.wait_ge(sem("y_ln"), 2 * g + 1)
                f(arena(QE_ + g * T, T), arena(QE_ + g * T, T), ACT.Exp, scale=-0.5)\
                    .then_inc(sem("y_ln"), 1)
            act.preload_act_table_set("silu_and_others")
            for j in range(3):
                gated(3, j)
            mixed = arena(16 * T, 16, T)
            for j in range(2):
                act.wait_ge(sem("z_step"), 4 + 9 + j)
                act_split(0, j, WO_A, WO_N, mixed)
            gated(3, 3)
            act.wait_ge(sem("z_step"), 20)
            for t in range(NT):
                act.dma_start(X1[:, t, :], x_rows[t]).then_inc(sem("x_again"), 16)
            act.dma_start(WB, a["post_mix_norm"].to_broadcast([P, D])).then_inc(sem("x_again"), 16)
            down(WO_N, WO_A, 16, mixed, ("y_norm", lambda k: 8), begun=2)

            def squares(n0, count, tiles_):
                for t in range(NT):
                    if t < NT - 1:
                        act.wait_ge(sem("rows_done"), (NT - 1) * (tiles_ // NT) + t + 1)
                    else:
                        used(0, n0 + count - 1)
                    f(XN[:, t, :], PS[:, 2 * t:2 * t + 2, :].rearrange("p a b -> p (a b)"), ACT.Square,
                      accum_out=sumsq2[:, tiles_ + t:tiles_ + t + 1]).then_inc(sem("p_square"), 1)

            squares(WO_N, 16, 0)
            norm(1, X1, NT, 4, ("x_res", 1))
            split(0, UP_N + 1)
            norm_high(1, NT, lambda k: PAR[:, 2, 88 + k:89 + k])
            act.preload_act_table_set("silu_and_others")

            def up_split(q, j):
                act.wait_ge(sem(f"w_in{j % 4}"), 16 * q + 16 * ((UP_N + j) // 4 + 1))
                act.wait_ge(sem("w_used"), 4 * q + UP_N + j + (0 if j % 4 > 1 else -1))
                f(parts(j)[0], RAW[:, j % 4, :], ACT.Copy).then_inc(sem("w_high"), 1)

            def ffn(q, i, j, cg):
                up_split(q, j + 3)
                if j < 2:
                    used(q, UP_N + j)
                if j == 0:
                    f(CT[:, 0, :], PS[:, 0, :], ACT.Copy, scale=PAR[:, 3, ds(q, 1)])\
                        .then_inc(sem("ffn_tap"), 1)
                    act.wait_ge(sem("ffn_step"), 5 * q + 5 + 2)
                    f(GT_T, CT[:, 0, :], ACT.Silu, bias=PAR[:, 3, ds(q + 44, 1)]).then_inc(sem("ffn_gate"), 1)
                elif j == 1:
                    f(CT[:, 1, :], PS[:, 1, :], ACT.Identity, scale=PAR[:, 3, ds(q + 22, 1)],
                      bias=PAR[:, 3, ds(q + 66, 1)]).then_inc(sem("ffn_tap"), 1)
                elif i == 3 and j == 3:
                    mod_rows(q, j, cg)

            def mod_rows(q, j, cg):
                used(q, UP_N + j)
                act.wait_ge(sem("mod_turned"), cg + 1)
                f(MR, PS[0:4, 4:6, :].rearrange("p a b -> p (a b)"), ACT.Copy)\
                    .then_inc(sem("mod_rows"), 1)

            up_split(0, 2)
            up_groups(act, ffn)
            up_split(0, 4 * FF + 3)
            split(0, DN_N)
            split(0, DN_N + 1)
            mod_rows(FF, 3, 5)
            for j in range(2):
                act_split(0, j, DN_A, DN_N, FFT)
            act.wait_ge(sem("mod_out"), 1)
            act.wait_ge(sem("x_res"), 4)
            with nc.allow_non_contiguous_dma(reason="16 KB of modulation, once"):
                for v, first in enumerate((16, 40)):
                    act.dma_start(gmod[v].rearrange("(t p) -> p t", p=P), modT[:, first:first + 8, 0])\
                        .then_inc(sem("gmod_out"), 16)
            act.dma_start(WB, a["post_ffn_norm"].to_broadcast([P, D])).then_inc(sem("wb_in"), 16)
            down(DN_N, DN_A, FF, FFT, ("ffn_step", lambda k: 5 * k + 5 + 5), begun=2)
            squares(DN_N, FF, 4)
            norm(2, X1, NT, 8, ("x_res", 5))
            split(0, PR_N + 1)
            for t in range(2):
                act.dma_start(arena(QT_, 2, D)[:, t, :], ctx_rows[t]).then_inc(sem(f"c_in{t}"), 16)
            act.wait_ge(sem("pad_out"), 16)
            act.dma_start(A[:, C2_:C2_ + 576], cst[:, COLMASK:FLIP]).then_inc(sem("c2_in"), 16)
            act.dma_start(FLP, cst[:, FLIP:NCST]).then_inc(sem("c2_in"), 16)
            norm(3, arena(QT_, 2, D), 2, 12, ("c_in",))
            act.wait_ge(sem("affine"), 1)
            norm_high(2, NT, lambda k: affine[:, 0, k:k + 1], lambda k: modT[:, k, 0:1])
            act.wait_ge(sem("n_turned"), 24)
            for v in range(2):
                act.dma_start(arena(R1_ + 4096, 2, NT, T)[:, v], dft[v].rearrange("(k p) t -> p k t", p=P))\
                    .then_inc(sem("dft_in"), 16)
            norm_high(3, 2, lambda k: affine[:, 1, k:k + 1], lambda k: modT[:, k, 1:2])
            for j in range(4):
                split(0, PR_N + j + 2)
                used(0, PR_N + j)
                f(arena(F_ + j * T, T), PS[:, j, :], ACT.Copy).then_inc(sem("pr_out"), 1)
            for part in range(3):
                for b in range(4):
                    split(0, PR_N + 4 + 4 * part + b + 2)
                used(0, PR_N + 4 + 4 * part + 3)
                for i in range(4 if part == 0 else 6):
                    at = [QK_, QK_ + 4 * T, V_][part] + i * T
                    f(arena(at, T), PS[:, BANKS[part][i][0], :], ACT.Copy).then_inc(sem("pr_out"), 1)
            for i in range(8):
                t, u = divmod(i, 2)
                act.wait_ge(sem("f_mix"), i + 1)
                f(arena(R1_ + t * 1024 + u * 512, 512), PS[:, 2 * (t % 2) + u, :], ACT.Copy)\
                    .then_inc(sem("f_mix_out"), 1)
            for gr in range(4):
                act.wait_ge(sem("f_done"), gr + 1)
                f(arena(F_ + gr * T, T), PS[:, 4 + gr, :], ACT.Copy).then_inc(sem("f_out"), 1)
            QT = arena(QT_, 4, T)
            KT = arena(KT_, 4, NKEY)
            for i in range(10):
                act.wait_ge(sem("qk_turned"), i + 1)
                src = PS[:, i % 4, :].rearrange("p (h t) -> p h t", t=P)
                dst = QT[:, :, i * P:(i + 1) * P] if i < 4 else KT[:, :, (i - 4) * P:(i - 3) * P]
                f(dst, src, ACT.Copy).then_inc(sem("qk_turned_out"), 1)
            act.preload_act_table_set("exp_and_others")

            def side_out(i):
                h, t = divmod(i, NT)
                act.wait_ge(sem("at_p_turned"), i + 1)
                if h > 1:
                    act.wait_ge(sem("at_o"), h - 1)
                f(probs_t(h)[:, 4:6, t * P:(t + 1) * P], turned(i)[1].rearrange("p (a b) -> p a b", b=P),
                  ACT.Copy).then_inc(sem("at_ctx_out"), 1)

            def head_out(h):
                act.wait_ge(sem("at_o"), h + 1)
                r = slice(DH * (h % 2), DH * (h % 2) + DH)
                f(QT[r, h // 2, :], PS[r, 7, :], ACT.Copy).then_inc(sem("at_o_out"), 1)

            for i in range(AH_ * NT):
                act.wait_ge(sem("at_max"), i + 1)
                if i > 1:
                    act.wait_ge(sem("at_p_turned"), i - 1)
                b = 2 * (i % 2)
                f(probs(i), PSF[:, b * 512:b * 512 + NKEY], ACT.Exp, bias=smax[:, i:i + 1],
                  accum_out=ssum[:, i:i + 1]).then_inc(sem("at_exp"), 1)
                if i:
                    side_out(i - 1)
                if i > NT and i % NT == 1:
                    head_out(i // NT - 1)
            side_out(AH_ * NT - 1)
            head_out(AH_ - 1)
            act.wait_ge(sem("at_o_out"), AH_)
            act.preload_act_table_set("sigmoid_and_others")

            def gate(g, j):
                split(g, GT_N + j + 2)
                used(g, GT_N + j)
                f(arena(R1_, 16, T)[:, 4 * g + j, :], PS[:, j, :], ACT.Sigmoid).then_inc(sem("gate_out"), 1)

            for k in range(4):
                f(AH[:, k, :], arena(F_ + k * T, T), ACT.Copy).then_inc(sem("branch_high"), 1)
            blocks(act, 16, gate)
            for k in range(4):
                f(HH[:, k, :], QT[:, k, :], ACT.Copy).then_inc(sem("branch_high"), 1)
            for n in range(7):
                split(0, FA_N + n + 2)
            used(0, W2_N - 2)
            for j in range(2):
                act.wait_ge(sem("merge_out"), j + 1)
                act_split(0, j, W2_A, W2_N, arena(MT_, 8, T))
            split(0, W2_N + 1)
            act.wait_ge(sem("x_res"), 8)
            act.wait_ge(sem("gmod_out"), 32)
            act.dma_start(WB, gmod[0:1, :].to_broadcast([P, D])).then_inc(sem("wb_in"), 16)
            down(W2_N, W2_A, 8, arena(MT_, 8, T), ("merge_out", lambda k: k + 1 if isinstance(k, int) else 8), begun=2)
            act.preload_act_table_set("exp_and_others")
            norm(4, X1, NT, 14, ("x_res", 9))
            split(0, M1_N + 1)
            act.dma_start(WB, gmod[1:2, :].to_broadcast([P, D])).then_inc(sem("wb_in"), 16)
            norm_high(4, NT, lambda k: affine[:, 2, k:k + 1], lambda k: modT[:, 24 + k, 0:1])

            def mlp(g, j):
                last = isinstance(g, int) and g == MF // 4 - 1 and j == 3
                if last:
                    for i in range(2):
                        act.wait_ge(sem("mlp_out"), 4 + i + 1)
                        act_split(0, i, M2_A, M2_N, arena(M1_, MF, T))
                else:
                    split(g, M1_N + j + 2)
                used(g, M1_N + j)
                act.wait_ge(sem("mlp_out"), 4 * g + j + 3)
                f(CT[:, j % 2, :], PS[:, j, :], ACT.Relu).then_inc(sem("mlp_relu"), 1)

            blocks(act, MF, mlp, whole=1)
            split(0, M2_N + 1)
            down(M2_N, M2_A, MF, arena(M1_, MF, T), ("mlp_out", lambda k: MF + 4), begun=2)

        @block.vector
        def _(dve):
            tt, ts, stt = dve.tensor_tensor, dve.tensor_scalar, dve.scalar_tensor_tensor
            own = [0]

            def step(ins):
                own[0] += 1
                ins.then_inc(sem("dve_own"), 1)
                dve.wait_ge(sem("dve_own"), own[0])

            dve.memset(half, -0.5).then_inc(sem("half"), 1)
            dve.memset(eps_col, EPS)
            dve.sem_inc(sem("w_low"), 4)
            dve.sem_inc(sem("w_used"), 2)
            dve.sem_inc(sem("conv_step"), 12)
            dve.sem_inc(sem("qk_sum"), 4)
            dve.sem_inc(sem("z_step"), 4)
            dve.sem_inc(sem("ffn_step"), 5)
            dve.sem_inc(sem("mlp_out"), 4)
            dve.sem_inc(sem("gate_out"), 4)

            def split(g, off):
                dve.wait_ge(sem("w_high"), 4 * g + off + 1)
                tt(WL[:, off % 2, :], RAW[:, off % 4, :], WH[:, off % 2, :].bitcast(F32),
                   ALU.subtract).then_inc(sem("w_low"), 1)

            def used(g, off):
                dve.wait_ge(sem("w_used"), 4 * g + off + 1 + 2)

            def act_split(g, j, a0, src):
                dve.wait_ge(sem("a_high"), 4 * g + j + a0 + 1)
                r = (a0 + j) % 4
                tt(AL[:, r, :], src[:, 4 * g + j, :], AH[:, r, :].bitcast(F32), ALU.subtract)\
                    .then_inc(sem("a_low"), 1)

            def scaled(job, x, xn, nt, tiles):
                for t in range(nt):
                    dve.wait_ge(sem("n_rstd"), tiles + t + 1)
                    ts(xn[:, t, :], x[:, t, :], rstd[:, tiles + t:tiles + t + 1], None, ALU.mult)\
                        .then_inc(sem("n_x"), 1)

            def norm_low(job, nt, gain, shift=None):
                hh, hl = HH, HL
                if job == 3:
                    hh, hl = (v[:, :, :].rearrange("p a b -> p (a b)").rearrange("p (k t) -> p k t", t=CTX)
                              for v in (AH, AL))

                if shift is None:
                    for k in range(KD):
                        dve.wait_ge(sem("n_high"), 8 * job + k + 1)
                        stt(hl[:, k, :], PS[:, 4 + k % 4, 0:nt * P], gain(k), hh[:, k, :].bitcast(F32),
                            ALU.mult, ALU.subtract).then_inc(sem("n_low"), 1)
                    return

                def low(k):
                    dve.wait_ge(sem("n_high"), 8 * job + k + 1)
                    tt(hl[:, k, :], HT[:, k % 2, 0:nt * P], hh[:, k, :].bitcast(F32), ALU.subtract)\
                        .then_inc(sem("n_low"), 1)

                for k in range(KD):
                    if k % 2 == 0:
                        dve.wait_ge(sem("n_turned"), 8 * job + k + 1)
                        dve.wait_ge(sem("n_low"), 8 * job + k - 1)
                        ts(HT[:, 0, 0:nt * P], PS[:, 4 + k % 4, 0:nt * P], gain(k), shift(k),
                           ALU.mult, ALU.add).then_inc(sem("n_even"), 1)
                    if k:
                        low(k - 1)
                low(KD - 1)

            def down(n0, a0, n, src, begun=0):
                for j in range(begun, 2):
                    act_split(0, j, a0, src)

                def body(g, j):
                    if not isinstance(g, int) or 4 * g + j + 2 < n:
                        act_split(g + (j + 2) // 4, (j + 2) % 4, a0, src)
                    if not isinstance(g, int) or (4 * g + j + 1 < n and n0 + 4 * g + j + 2 < END_N):
                        split(g, n0 + j + 2)

                blocks(dve, n, body, whole=1)

            def residual(f0, n0, count, wb, normed):
                dve.wait_ge(sem(wb[0]), wb[1])
                for t in range(NT):
                    if t < NT - 1:
                        dve.wait_ge(sem("rows_done"), (NT - 1) * f0 + t + 1)
                    else:
                        used(0, n0 + count - 1)
                    o = PS[:, 2 * t:2 * t + 2, :].rearrange("p a b -> p (a b)")
                    if t:
                        dve.wait_ge(sem("x_res"), NT * f0 + t)
                    if normed is not None:
                        dve.wait_ge(sem("p_rstd"), normed + t + 1)
                        step(stt(YT, o, rstd2[:, normed + t:normed + t + 1], WB, ALU.mult, ALU.mult))
                    else:
                        step(tt(YT, o, WB, ALU.mult))
                    tt(X1[:, t, :], X1[:, t, :], YT, ALU.add).then_inc(sem("x_res"), 1)

            dve.wait_ge(sem("params_turned"), 1)
            for s, r in enumerate(STAGED):
                dve.tensor_copy(PAR[:, s, 0:r], PS[:, s // 4, (s % 4) * P:(s % 4) * P + r])\
                    .then_inc(sem("params_out"), 1)
            dve.wait_ge(sem("params_out"), 5)
            for k in range(4):
                dve.tensor_copy(CW[:, k * CH:k * CH + 24], PAR[:, 0, k * 24:(k + 1) * 24])
                dve.tensor_copy(CW[:, k * CH + 24:(k + 1) * CH], PAR[:, 1, k * 12:(k + 1) * 12])
            dve.memset(CW[:, 4 * CH:4 * CH + 24], 0.0)
            step(dve.tensor_copy(CW[:, 4 * CH + 24:5 * CH], PAR[:, 1, 48:60]))
            scaled(0, XN, XN, NT, 0)
            split(0, 0)
            dve.wait_ge(sem("small_high"), 2)
            tt(CD4[:, :, 2:4], cond, CD4[:, :, 0:2].bitcast(F32), ALU.subtract)
            tt(join, IDN[0:4, 0:2], IDN[0:4, 2:4], ALU.add).then_inc(sem("join_ready"), 1)
            tt(SL[:, :, :], small_w, SH[:, :, :].bitcast(F32), ALU.subtract).then_inc(sem("small_low"), 1)
            split(0, 1)
            norm_low(0, NT, lambda k: PAR[:, 1, 60 + k:61 + k])

            def conv(g, j):
                i = 4 * g + j
                split(g, CONV_N + j + 2)
                for k in range(3):
                    lag = k + 1
                    if k == 0:
                        dve.wait_ge(sem("tap"), i + 1)
                    else:
                        dve.wait_ge(sem("conv_step"), 12 + 3 * i + k)
                    o = CT[:, j % 2, lag:T]
                    stt(o, PS[:, j, 0:T - lag], CW[:, ds((3 - lag) * CH + i, 1)], o, ALU.mult, ALU.add)\
                        .then_inc(sem("conv_step"), 1)

            def square(g, j):
                dve.wait_ge(sem("qk_sum"), 4 * g + j + 1)
                dve.wait_ge(sem("conv_out"), 4 * g + j + 1)
                tt(arena(QE_ + (j % 4) * T, T), FT[:, 4 * g + j, :], FT[:, 4 * g + j, :], ALU.mult)\
                    .then_inc(sem("qk_square"), 1)

            def conv_qk(g, j):
                if j or not isinstance(g, int) or g:
                    square(g, j - 1)
                conv(g, j)

            for j in range(4):
                conv_qk(0, j)
            dve.wait_ge(sem("proj_done"), 1)
            step(dve.tensor_copy(proj, PS[:, 7, 0:P].rearrange("p (a b) -> p a b", b=32)))
            step(tt(sp_x, proj[:, :, 8:32], each(head_bias, NT), ALU.add))
            step(ts(sp_q, sp_x, -1.0, None, ALU.mult))
            tt(sp_e, sp_x, sp_q, ALU.max).then_inc(sem("sp_abs"), 1)
            for j in range(4):
                conv_qk(1, j)
            dve.wait_ge(sem("sp_exp"), 3)
            step(ts(sp_s, sp_e, 2.0, None, ALU.add))
            step(dve.reciprocal(sp_s, sp_s))
            step(tt(sp_s, sp_s, sp_e, ALU.mult))
            step(tt(sp_q, sp_s, sp_s, ALU.mult))
            step(ts(soft, sp_q, 1.0 / 17, 1.0 / 15, ALU.mult, ALU.add))
            for n in (13, 11, 9, 7, 5, 3, 1):
                step(tt(soft, soft, sp_q, ALU.mult))
                step(ts(soft, soft, 1.0 / n, None, ALU.add))
            step(tt(soft, soft, sp_s, ALU.mult))
            step(ts(sp_x, sp_x, 0.0, None, ALU.max))
            step(stt(soft, soft, 2.0, sp_x, ALU.mult, ALU.add))
            step(ts(nega, nega, -1.0, None, ALU.mult))
            step(tt(logdec, soft, each(nega, NT), ALU.mult))
            step(ts(beta, beta, 1.0, None, ALU.add))
            dve.reciprocal(beta, beta).then_inc(sem("logdec_ready"), 1)
            dve.wait_ge(sem("logdec_ready"), 1)
            with dve.Fori(2, 4) as g:
                for j in range(4):
                    conv_qk(g, j)
            square(4, -1)
            for j in range(4):
                conv(4, j)
            for j in range(4):
                conv(5, j)
            dve.wait_ge(sem("cum_done"), 1)
            cum = PS[:, 4, 0:96].rearrange("p (a b) -> p a b", b=24)
            step(ts(ncum, cum, -1.0, None, ALU.mult))
            tt(edec, PS[:, 5, 0:96].rearrange("p (a b) -> p a b", b=24), ncum, ALU.add)\
                .then_inc(sem("cum_out"), 1)
            dve.wait_ge(sem("qk_sum"), 4 + 16)
            ts(qks, PS[:, 6, 0:2 * 64].rearrange("p (a b) -> p a b", b=2)[:, :, 0]
               .rearrange("p (a b) -> p a b", b=16), EPS, None, ALU.add).then_inc(sem("qk_eps"), 1)
            with dve.Fori(6, 8) as g:
                for j in range(4):
                    conv(g, j)
            dve.wait_ge(sem("qk_pow"), 1)
            dve.wait_ge(sem("cum_exp"), 3)
            rk = qkr[:, :, 8:16]
            ts(nrk, rk, -1.0, None, ALU.mult)
            step(tt(brk, rk, beta, ALU.mult))
            tt(kbs, brk, ecum[:, :, 0:8], ALU.mult)
            tt(kds, rk, edec[:, :, 0:8], ALU.mult)
            step(ts(qkr[:, :, 0:8], qkr[:, :, 0:8], float(P) ** -0.5, None, ALU.mult))
            step(tt(rq2, qkr[:, :, 0:8], qkr[:, :, 0:8], ALU.mult))
            ts(rq2, rq2, 1.0 / P, None, ALU.mult).then_inc(sem("scales_ready"), 1)
            for j in range(4):
                conv(8, j)
            dve.wait_ge(sem("scales_ready"), 1)
            dve.wait_ge(sem("levels_in"), 1)

            def four(q):
                return range(4 * q, 4 * q + 4)

            def tiles(at, q):
                return arena(at + q * 512, 4, P)

            def bank(b):
                return PS[:, b, :].rearrange("p (h t) -> p h t", t=P)

            def heads(v, c, q):
                return up_to(v[:, c, 4 * q:4 * q + 4], 4)

            for c in range(NT):
                tc = slice(c * P, (c + 1) * P)
                for q in range(2):
                    dve.wait_ge(sem("d_cum"), 2 * c + q + 1)
                    tt(tiles(PP_, q), bank(q), each(NGM, 4), ALU.add).then_inc(sem("d_arg"), 1)
                for q in range(2):
                    dve.wait_ge(sem("d_exp"), 2 * c + q + 1)
                    dve.wait_ge(sem("d_gram"), 2 * c + q + 1)
                    step(tt(tiles(NM_, q), tiles(PP_, q), bank(2 + q), ALU.mult))
                    for h in four(q):
                        hc = slice((h % 4) * P, (h % 4 + 1) * P)
                        stt(arena(NM_ + h * P, P), PS[:, 4 + q, hc], nrk[:, c, h:h + 1],
                            arena(NM_ + h * P, P), ALU.mult, ALU.mult)
                        m = stt(arena(QE_ + h * P, P), PS[:, 6 + q, hc], rk[:, c, h:h + 1],
                                arena(PP_ + h * P, P), ALU.mult, ALU.mult)
                    step(m)
                    step(dve.tensor_copy(tiles(R_, q), each(IDN, 4)))
                    dve.copy_predicated(tiles(R_, q), each(LV[:, 1, :], 4), tiles(NM_, q))\
                        .then_inc(sem("d_r0"), 1)
                for q in range(2):
                    dve.wait_ge(sem("d_r0_turned"), 2 * c + q + 1)
                    dve.tensor_copy(tiles(TT_, q), bank(q)).then_inc(sem("d_level"), 1)
                for level in range(1, LEVELS):
                    u = 2 * (c * (LEVELS - 1) + level - 1) + 1
                    for q in range(2):
                        dve.wait_ge(sem("d_tnt"), u + q)
                        if level < LEVELS - 1:
                            dve.copy_predicated(tiles(TT_, q), each(LV[:, 2 * level, :], 4), bank(4 + q))
                        dve.copy_predicated(tiles(R_, q), each(LV[:, 2 * level + 1, :], 4), bank(6 + q))\
                            .then_inc(sem("d_level"), 1)
                for q in range(2):
                    dve.wait_ge(sem("d_kv_turned"), 2 * c + q + 1)
                    tt(tiles(TT_, q), bank(q), heads(kbs, c, q), ALU.mult)
                    tt(tiles(NM_, q), bank(q), heads(kds, c, q), ALU.mult)
                    tt(tiles(PP_, q), bank(2 + q), heads(beta, c, q), ALU.mult).then_inc(sem("d_kv_out"), 1)
                for q in range(2):
                    dve.wait_ge(sem("d_out"), 2 * c + q + 1)
                    if c:
                        step(tt(tiles(R_, q), bank(q), heads(ecum, c, q), ALU.mult))
                        tt(tiles(R_, q), tiles(R_, q), bank(2 + q), ALU.add).then_inc(sem("d_o"), 1)
                        for h in four(q):
                            m = stt(arena(SD_ + h * P, P), arena(SD_ + h * P, P), etot[:, c, h:h + 1],
                                    PS[:, 4 + q, (h % 4) * P:(h % 4 + 1) * P], ALU.mult, ALU.add)
                    else:
                        dve.tensor_copy(tiles(R_, q), bank(2 + q)).then_inc(sem("d_o"), 1)
                        m = dve.tensor_copy(tiles(SD_, q), bank(4 + q))
                    m.then_inc(sem("d_state"), 1)
                for q in range(2):
                    hs = slice(4 * q, 4 * q + 4)
                    dve.wait_ge(sem("d_o_square"), 2 * c + q + 1)
                    step(dve.tensor_reduce(oss[:, c, hs], tiles(PP_, q), AX.X, ALU.add))
                    step(tt(oss[:, c, hs], oss[:, c, hs], rq2[:, c, hs], ALU.mult))
                    ts(oss[:, c, hs], oss[:, c, hs], EPS, None, ALU.add).then_inc(sem("o_eps"), 1)
                def wide(v, lo):
                    return v[:, c, lo:lo + HS].unsqueeze(2).to_broadcast([P, HS, PD])

                xt = PS[:, 0:2, :].rearrange("p a b -> p (a b)").rearrange("p (h d) -> p h d", d=PD)
                dve.wait_ge(sem("s_turned"), c + 1)
                tt(arena(TT_, HS, PD), xt, wide(soft, 8), ALU.mult)
                for q in range(2):
                    hs = slice(4 * q, 4 * q + 4)
                    dve.wait_ge(sem("o_pow"), 2 * c + q + 1)
                    step(tt(ors[:, c, hs], ors[:, c, hs], qkr[:, c, hs], ALU.mult))
                    tt(tiles(R_, q), tiles(R_, q), heads(ors, c, q), ALU.mult).then_inc(sem("d_normed"), 1)

                def arguments(g):
                    dve.wait_ge(sem("s_cum"), 2 * c + g + 1)
                    for r in range(2):
                        m = tt(tiles([QE_, R_][g], r), bank(4 + 2 * g + r), each(NGM, 4), ALU.add)
                    m.then_inc(sem("s_arg"), 1)

                arguments(0)
                tt(arena(NM_, HS, PD), arena(TT_, HS, PD), wide(edec, 8), ALU.mult)
                tt(arena(PP_, HS, PD), xt, skip_d.unsqueeze(2).to_broadcast([P, HS, PD]), ALU.mult)
                dve.wait_ge(sem("d_o_turned"), 2 * c + 2)
                arguments(1)
                for g in range(2):
                    dve.wait_ge(sem("s_exp"), 2 * c + g + 1)
                    for r in range(2):
                        o = tiles([QE_, R_][g], r)
                        m = tt(o, o, each(PS[:, 3, g * P:(g + 1) * P], 4), ALU.mult)
                    m.then_inc(sem("s_m"), 1)
                for g in range(2):
                    dve.wait_ge(sem("s_sum"), 2 * c + g + 1)
                    y, xd = arena(VN_ + g * 512, 8, PD), arena(PP_ + g * 512, 8, PD)
                    st = arena(SS_ + g * 512, 8, PD)

                    def rate(v):
                        return v[:, c, 8 + 8 * g:16 + 8 * g].unsqueeze(2).to_broadcast([P, 8, PD])

                    def whole(b):
                        return PS[:, b, :].rearrange("p (h d) -> p h d", d=PD)

                    step(tt(y, whole(4 + 2 * g), xd, ALU.add))
                    if c:
                        step(tt(xd, whole(5 + 2 * g), rate(ecum), ALU.mult))
                        tt(y, y, xd, ALU.add)
                        step(tt(st, st, rate(etot), ALU.mult))
                        m = tt(st, st, whole(g), ALU.add)
                    else:
                        m = dve.tensor_copy(st, whole(g))
                    m.then_inc(sem("s_y"), 1)

            mixed = arena(16 * T, 16, T)

            def gated(g, j):
                i = 4 * g + j
                if i < 15:
                    split(g, Z_N + j + 2)
                else:
                    for k in range(2):
                        act_split(0, k, WO_A, mixed)
                dve.wait_ge(sem("z_silu"), i + 1)
                src, dst = (X0 + i, X0 + i) if i < 8 else (i - 8, i + 8)
                tt(FT[:, dst, :], FT[:, src, :], arena(R_ + j * T, T), ALU.mult).then_inc(sem("z_step"), 1)

            for g in range(3):
                for j in range(4):
                    gated(g, j)
            for i in range(8):
                if i % 4 == 0:
                    dve.wait_ge(sem("y_ln"), 2 * (i // 4) + 2)
                stt(FT[:, X0 + i, :], FT[:, X0 + i, :], PAR[:, 1, 69 + i:70 + i], arena(QE_ + (i // 4) * T, T),
                    ALU.mult, ALU.mult).then_inc(sem("y_norm"), 1)
            for j in range(4):
                gated(3, j)
            split(0, WO_N + 1)
            down(WO_N, WO_A, 16, mixed, begun=2)
            residual(0, WO_N, 16, ("x_again", 80), 0)
            dve.memset(MR, 0.0).then_inc(sem("mod_rows"), 1)
            scaled(1, X1, XN, NT, 4)
            split(0, UP_N + 1)
            norm_low(1, NT, lambda k: PAR[:, 2, 88 + k:89 + k])

            def up_split(q, j):
                dve.wait_ge(sem("w_high"), 4 * q + UP_N + j + 1)
                wh, wl = parts(j)
                tt(wl, RAW[:, j % 4, :], wh.bitcast(F32), ALU.subtract).then_inc(sem("w_low"), 1)

            def ffn(q, i, j, cg):
                up_split(q, j + 3)
                base = 5 * q + 5
                if j < 2:
                    dve.wait_ge(sem("ffn_tap"), 2 * q + j + 1)
                    for lag in (1, 2):
                        if lag == 2:
                            dve.wait_ge(sem("ffn_step"), base + 2 * j + 1)
                        o = CT[:, j, lag:T]
                        w = PAR[:, 2, ds(q + (2 - lag) * 2 * FF + j * FF, 1)]
                        stt(o, PS[:, j, 0:T - lag], w, o, ALU.mult, ALU.add).then_inc(sem("ffn_step"), 1)
                if j == 1:
                    dve.wait_ge(sem("ffn_gate"), q + 1)
                    dve.wait_ge(sem("ffn_step"), base + 4)
                    tt(FFT[:, q, :], CT[:, 1, :], GT_T, ALU.mult).then_inc(sem("ffn_step"), 1)

            up_split(0, 2)
            up_groups(dve, ffn)
            up_split(0, 4 * FF + 3)
            split(0, DN_N)
            split(0, DN_N + 1)
            for j in range(2):
                act_split(0, j, DN_A, FFT)
            dve.wait_ge(sem("mod_turned"), 7)
            tt(modT, PS[:, 6, 2 * KD:2 * KD + 2 * NADA].rearrange("p (a b) -> p a b", b=2),
               PAR[:, 4, 0:NADA].unsqueeze(2).to_broadcast([P, NADA, 2]), ALU.add).then_inc(sem("mod_out"), 1)
            dve.wait_ge(sem("mod_out"), 1)
            for r, (gain, scale, who) in enumerate(((48, 8, 0), (48, 8, 1), (56, 32, 0))):
                stt_in = modT[:, scale:scale + 8, who]
                step(stt(affine[:, r, :], stt_in, 1.0, PAR[:, 4, gain:gain + 8], ALU.add, ALU.mult))
            dve.sem_inc(sem("affine"), 1)
            down(DN_N, DN_A, FF, FFT, begun=2)
            residual(1, DN_N, FF, ("wb_in", 16), 4)
            XC = arena(QT_, 2, D)
            scaled(2, X1, XN, NT, 8)
            split(0, PR_N + 1)
            scaled(3, XC, XC, 2, 12)
            norm_low(2, NT, lambda k: affine[:, 0, k:k + 1], lambda k: modT[:, k, 0:1])
            norm_low(3, 2, lambda k: affine[:, 1, k:k + 1], lambda k: modT[:, k, 1:2])
            QK = arena(QK_, 10, AH_, DH)
            COS = arena(C2_ + 320, NT, 2, 16)
            SIN = arena(C2_ + 448, NT, 2, 16)
            sq = arena(QS_, AH_, DH)

            def mean_square(i):
                dve.wait_ge(sem("pr_out"), i + 5)
                step(tt(sq, QK[:, i], QK[:, i], ALU.mult))
                step(dve.tensor_reduce(qkss[:, i, :], sq, AX.X, ALU.add))
                ts(qkss[:, i, :], qkss[:, i, :], 1.0 / DH, EPS, ALU.mult, ALU.add).then_inc(sem("qk_ms"), 1)

            def normed(i):
                gain = qkg[:, 0:DH] if i < 4 else qkg[:, DH:2 * DH]
                dve.wait_ge(sem("qk_rstd"), i + 1)
                step(tt(QK[:, i], QK[:, i], qkrs[:, i, :].unsqueeze(2).to_broadcast([P, AH_, DH]), ALU.mult))
                m = tt(QK[:, i], QK[:, i], gain.unsqueeze(1).to_broadcast([P, AH_, DH]), ALU.mult)
                if i < 8:
                    step(m)
                    v = QK[:, i].rearrange("p h (a s d) -> p h a s d", a=2, s=2)
                    x0, x1 = v[:, :, :, 0, :], v[:, :, :, 1, :]
                    cs, sn = (w[:, i % 4].unsqueeze(1).to_broadcast([P, AH_, 2, 16]) for w in (COS, SIN))
                    a0 = arena(QS_, AH_, 32).rearrange("p h (a d) -> p h a d", a=2)
                    a1 = arena(QS_ + 256, AH_, 32).rearrange("p h (a d) -> p h a d", a=2)
                    tt(a0, x0, sn, ALU.mult)
                    step(tt(a1, x1, sn, ALU.mult))
                    step(tt(x0, x0, cs, ALU.mult))
                    step(tt(x1, x1, cs, ALU.mult))
                    tt(x0, x0, a1, ALU.subtract)
                    m = tt(x1, x1, a0, ALU.add)
                m.then_inc(sem("qk_ready"), 1)
                dve.wait_ge(sem("qk_ready"), i + 1)

            for n in range(16):
                split(0, PR_N + n + 2)
                if n == 8:
                    dve.wait_ge(sem("c2_in"), 32)
                    dve.wait_ge(sem("qkg_in"), 32)
                if n >= 8:
                    mean_square(n - 8)
                if n > 8:
                    normed(n - 9)
            mean_square(8)
            normed(7)
            mean_square(9)
            normed(8)
            normed(9)
            for i in range(AH_ * NT + 2):
                if 0 < i < AH_ * NT + 1:
                    k = i - 1
                    dve.wait_ge(sem("at_exp"), k + 1)
                    step(dve.reciprocal(srec[:, k:k + 1], ssum[:, k:k + 1]))
                    ts(probs(k), probs(k), srec[:, k:k + 1], None, ALU.mult).then_inc(sem("at_scaled"), 1)
                if i < AH_ * NT:
                    b = 2 * (i % 2)
                    dve.wait_ge(sem("at_scores"), i + 1)
                    dve.tensor_reduce(smax[:, i:i + 1], PSF[:, b * 512:b * 512 + NKEY], AX.X, ALU.max,
                                      negate=True).then_inc(sem("at_max"), 1)
                if i > 1:
                    k = i - 2
                    h, t = divmod(k, NT)
                    dve.wait_ge(sem("at_p_turned"), k + 1)
                    if h > 1:
                        dve.wait_ge(sem("at_o"), h - 1)
                    dve.tensor_copy(probs_t(h)[:, 0:4, t * P:(t + 1) * P],
                                    turned(k)[0].rearrange("p (a b) -> p a b", b=P))\
                        .then_inc(sem("at_main_out"), 1)
            for k in range(4):
                dve.wait_ge(sem("branch_high"), k + 1)
                tt(AL[:, k, :], arena(F_ + k * T, T), AH[:, k, :].bitcast(F32), ALU.subtract)\
                    .then_inc(sem("branch_low"), 1)

            def gate(g, j):
                split(g, GT_N + j + 2)

            blocks(dve, 16, gate)
            for k in range(4):
                dve.wait_ge(sem("branch_high"), k + 5)
                tt(HL[:, k, :], arena(QT_, 4, T)[:, k, :], HH[:, k, :].bitcast(F32), ALU.subtract)\
                    .then_inc(sem("branch_low"), 1)
            G = arena(R1_, 16, T)
            MT = arena(MT_, 8, T)
            mg = arena(KT_, 2, T)
            for n in range(8):
                if n < 7:
                    split(0, FA_N + n + 2)
                else:
                    for j in range(2):
                        act_split(0, j, W2_A, MT)
                if n % 2:
                    used(0, FA_N + n)
                    for mm in range(2):
                        m = n - 1 + mm
                        if m:
                            dve.wait_ge(sem("merge_out"), m)
                        tt(mg[:, 0, :], PS[:, 2 * (m % 4), :], G[:, m, :], ALU.mult)
                        step(tt(mg[:, 1, :], PS[:, 2 * (m % 4) + 1, :], G[:, 8 + m, :], ALU.mult))
                        tt(MT[:, m, :], mg[:, 0, :], mg[:, 1, :], ALU.add).then_inc(sem("merge_out"), 1)
            split(0, W2_N + 1)
            down(W2_N, W2_A, 8, MT, begun=2)
            residual(2, W2_N, 8, ("wb_in", 32), None)
            scaled(4, X1, XN, NT, 14)
            split(0, M1_N + 1)
            norm_low(4, NT, lambda k: affine[:, 2, k:k + 1], lambda k: modT[:, 24 + k, 0:1])
            M1 = arena(M1_, MF, T)

            def mlp(g, j):
                if isinstance(g, int) and g == MF // 4 - 1 and j == 3:
                    for i in range(2):
                        act_split(0, i, M2_A, M1)
                else:
                    split(g, M1_N + j + 2)
                dve.wait_ge(sem("mlp_relu"), 4 * g + j + 1)
                tt(M1[:, 4 * g + j, :], CT[:, j % 2, :], CT[:, j % 2, :], ALU.mult)\
                    .then_inc(sem("mlp_out"), 1)

            blocks(dve, MF, mlp, whole=1)
            split(0, M2_N + 1)
            down(M2_N, M2_A, MF, M1, begun=2)
            residual(3, M2_N, MF, ("wb_in", 48), None)

        @block.gpsimd
        def _(pool):
            own = [0]

            def step(ins):
                own[0] += 1
                ins.then_inc(sem("pool_own"), 1)
                pool.wait_ge(sem("pool_own"), own[0])

            def rstds(tiles, n):
                for t in range(tiles, tiles + n):
                    pool.wait_ge(sem("n_square"), t + 1)
                    step(pool.tensor_scalar(meansq[:, t:t + 1], sumsq[:, t:t + 1], 1.0 / D, EPS,
                                            ALU.mult, ALU.add))
                    pool.tensor_tensor(rstd[:, t:t + 1], meansq[:, t:t + 1], half[:, 0:1], ALU.pow)\
                        .then_inc(sem("n_rstd"), 1)

            def rstds2(tiles):
                for t in range(tiles, tiles + 4):
                    pool.wait_ge(sem("p_square"), t + 1)
                    step(pool.tensor_scalar(meansq2[:, t:t + 1], sumsq2[:, t:t + 1], 1.0 / D, EPS,
                                            ALU.mult, ALU.add))
                    pool.tensor_tensor(rstd2[:, t:t + 1], meansq2[:, t:t + 1], half[:, 0:1], ALU.pow)\
                        .then_inc(sem("p_rstd"), 1)

            pool.wait_ge(sem("half"), 1)
            rstds(0, 4)
            pad = A[0:120, C2_:C2_ + P]
            step(pool.memset(pad, 0.0))
            pool.dma_start(pad[:, 48:79], a["rpb_2"][0].rearrange("h r c -> (h r) c"))\
                .then_inc(sem("pad_in"), 16)
            pool.wait_ge(sem("pad_in"), 16)
            pool.dma_start(gpad.rearrange("h r c -> (h r) c"), pad).then_inc(sem("pad_out"), 16)
            pool.wait_ge(sem("levels_raw"), 16)
            pool.tensor_copy(LV[:, :, :].rearrange("p a b -> p (a b)"), LVF).then_inc(sem("levels_in"), 1)
            pool.wait_ge(sem("qk_eps"), 1)
            pool.tensor_tensor(qkr, qks, half.rearrange("p (a b) -> p a b", b=16), ALU.pow)\
                .then_inc(sem("qk_pow"), 1)
            for i in range(2 * NT):
                c, q = divmod(i, 2)
                hs = slice(4 * q, 4 * q + 4)
                pool.wait_ge(sem("o_eps"), i + 1)
                pool.tensor_tensor(ors[:, c, hs], oss[:, c, hs], half[:, 0:4], ALU.pow)\
                    .then_inc(sem("o_pow"), 1)
            rstds2(0)
            rstds(4, 4)
            rstds2(4)
            rstds(8, 4)
            rstds(12, 2)
            for n, name in enumerate(("q_norm_g_2", "k_norm_g_2")):
                pool.dma_start(qkg[:, n * DH:(n + 1) * DH], a[name].to_broadcast([P, DH]))\
                    .then_inc(sem("qkg_raw"), 16)
            pool.wait_ge(sem("qkg_raw"), 32)
            pool.tensor_scalar(qkg[:, 0:DH], qkg[:, 0:DH], DH ** -0.5, 0.0, ALU.mult, ALU.add)\
                .then_inc(sem("qkg_in"), 32)
            for i in range(10):
                pool.wait_ge(sem("qk_ms"), i + 1)
                pool.tensor_tensor(qkrs[:, i, :], qkss[:, i, :], half[:, 0:AH_], ALU.pow)\
                    .then_inc(sem("qk_rstd"), 1)
            pool.wait_ge(sem("pad_out"), 16)
            pool.wait_ge(sem("f_done"), 4)
            for h in range(AH_):
                if h > 1:
                    pool.wait_ge(sem("at_scores"), NT * (h - 1))
                buf = arena(AG_ + (h % 2) * 1024, 16, GRID)
                for u in range(2):
                    src = bass.AP(gpad.tensor, h * 15 * P, [[1, GRID], [P, 15], [1, GRID]])
                    pool.dma_start(buf[u * GRID:(u + 1) * GRID, u:u + 15, :], src)\
                        .then_inc(sem(f"bias_in{h % 2}"), 16)
                pool.wait_ge(sem(f"bias_in{h % 2}"), 32 * (h // 2 + 1))
                pool.tensor_tensor(buf[:, 1:15, :], buf[:, 1:15, :],
                                   arena(C2_, GRID).unsqueeze(1).to_broadcast([P, 14, GRID]), ALU.add)\
                    .then_inc(sem("bias_ready"), 1)
            rstds(14, 4)


NAMES = ["x", "pre_mix_norm", "w_in", "gdn_conv_w", "gdn_a_log", "gdn_dt_bias", "gdn_norm_w",
         "ssd_conv_w", "ssd_conv_b", "ssd_a_log", "ssd_dt_bias", "ssd_d", "ssd_norm_w", "w_out",
         "post_mix_norm", "pre_ffn_norm", "w_up", "ffn_conv_w", "ffn_conv_b", "w_down",
         "post_ffn_norm", "c_2", "ctx_2", "c_ctx_2", "w_ada_2", "b_ada_2", "norm1_g_2", "norm2_g_2",
         "w_in_2", "q_norm_g_2", "k_norm_g_2", "rpb_2", "w_branch_gate_2", "w_fourier_out_2",
         "w_attn_out_2", "w_out_2", "w_mlp1_2", "w_mlp2_2"]


def kernel(**inputs):
    import concourse.bacc as bacc
    from concourse.bass_utils import run_bass_kernel_spmd

    nc = bacc.Bacc("TRN2", target_bir_lowering=False, num_devices=1)
    arrays, a = {}, {}
    for name in NAMES:
        arrays[name] = np.ascontiguousarray(inputs[name])
        a[name] = nc.dram_tensor(name, arrays[name].shape, F32, kind="ExternalInput").ap()
    for name, v in (("constants", constants()), ("transforms", transforms())):
        arrays[name] = v
        a[name] = nc.dram_tensor(name, v.shape, F32, kind="ExternalInput").ap()
    gmod = nc.dram_tensor("modulation_rows", (2, D), F32, kind="Internal").ap()
    gpad = nc.dram_tensor("padded_bias", (AH_, 15, P), F32, kind="Internal").ap()
    out = nc.dram_tensor("result", (1, T, D), F32, kind="ExternalOutput").ap()
    program(nc, a, a["constants"], a["transforms"], gmod, gpad, out)
    return run_bass_kernel_spmd(nc, [arrays], core_ids=[0]).results[0]["result"]
```
